# Optimizing a Trainium2 kernel written in Bass

```python
import jax, jax.numpy as jnp
from jax import lax
import numpy as np

D_MODEL = 1024
BATCH = 1
SEQ = 512
DEPTH = 2
DEC_BATCH = 8
DEC_SEQ = 4
PAST_LEN = 4096
PAGE_SIZE = 128

N_MIXERS = 2
N_RET_LAYERS = (DEPTH + 1) // 2
N_DN_LAYERS = DEPTH // 2
RET_HEADS = 4
RET_DK = D_MODEL // RET_HEADS
RET_DV = 2 * RET_DK
RET_QW = RET_HEADS * RET_DK
RET_VW = RET_HEADS * RET_DV
RET_IN = 2 * RET_QW + 2 * RET_VW
RET_CHUNK = 128
DN_QK_HEADS = 8
DN_V_HEADS = 16
DN_DK = 128
DN_DV = 128
DN_QW = DN_QK_HEADS * DN_DK
DN_VW = DN_V_HEADS * DN_DV
DN_CONV_CH = 2 * DN_QW + DN_VW
DN_IN = DN_CONV_CH + DN_VW + 2 * DN_V_HEADS
DN_CONV_W = 4
DN_CHUNK = 64
N_EXPERTS = 16
N_GROUPS = 4
EXPERTS_PER_GROUP = N_EXPERTS // N_GROUPS
TOP_K = 2
GROUP_SCORE_K = 2
D_EXPERT = D_MODEL // 4
N_MOD = 6
ALPHA = (2.0 * DEPTH) ** 0.25
BETA_INIT = (8.0 * DEPTH) ** -0.25
LN_EPS = 1e-5
F32 = jnp.float32

kernel_name = "hybrid_retention_gdn_groupmoe_step"

def _layer_norm(x, g, b):
    xf = x.astype(F32)
    mu = xf.mean(-1, keepdims=True)
    var = jnp.square(xf - mu).mean(-1, keepdims=True)
    return ((xf - mu) * lax.rsqrt(var + LN_EPS) * g.astype(F32) + b.astype(F32)).astype(x.dtype)

def _rms_norm(x, g):
    xf = x.astype(F32)
    return xf * lax.rsqrt(jnp.mean(xf * xf, -1, keepdims=True) + 1e-6) * g.astype(F32)

def _l2norm(x):
    return x * lax.rsqrt(jnp.sum(x * x, -1, keepdims=True) + 1e-6)

def _rotary(x, pos0):
    L, d = x.shape[1], x.shape[-1]
    half = d // 2
    inv_freq = 10000.0 ** (-jnp.linspace(0.0, 1.0, half, dtype=F32))
    pos = (pos0 + jnp.arange(L)).astype(F32)
    ang = pos[:, None] * inv_freq[None, :]
    cos = jnp.cos(ang)[None, :, None, :]
    sin = jnp.sin(ang)[None, :, None, :]
    x1 = x[..., :half].astype(F32)
    x2 = x[..., half:].astype(F32)
    return jnp.concatenate([x1 * cos - x2 * sin, x2 * cos + x1 * sin], axis=-1)

def _to_chunks(t, n, c):
    B, L, H = t.shape[:3]
    t = t.reshape((B, n, c, H) + t.shape[3:])
    return jnp.moveaxis(t, (1, 3), (0, 2))

def _from_chunks(t):
    n, B, H, c = t.shape[:4]
    t = jnp.moveaxis(t, (0, 2), (1, 3))
    return t.reshape((B, n * c, H) + t.shape[4:])

def _retention_chunked(q, k, v, s0):
    L = q.shape[1]
    c = min(RET_CHUNK, L)
    n = L // c
    lg = jnp.log(1.0 - 2.0 ** (-5.0 - jnp.arange(RET_HEADS, dtype=F32)))
    idx = jnp.arange(c, dtype=F32)
    diff = idx[:, None] - idx[None, :]
    decay_intra = jnp.exp(jnp.where(diff[None] >= 0, diff[None] * lg[:, None, None], -jnp.inf))
    q_dec = jnp.exp((idx + 1.0)[None, :] * lg[:, None])
    k_dec = jnp.exp((c - 1.0 - idx)[None, :] * lg[:, None])
    s_dec = jnp.exp(c * lg)

    def step(s, xs):
        qi, ki, vi = xs
        att = jnp.einsum('bhid,bhjd->bhij', qi, ki) * decay_intra
        o = (jnp.einsum('bhij,bhjv->bhiv', att, vi)
             + jnp.einsum('bhid,bhdv->bhiv', qi * q_dec[..., None], s))
        s = s * s_dec[:, None, None] + jnp.einsum('bhjd,bhjv->bhdv', ki * k_dec[..., None], vi)
        return s, o

    s, o = lax.scan(step, s0, (_to_chunks(q, n, c), _to_chunks(k, n, c), _to_chunks(v, n, c)))
    return _from_chunks(o), s

def _retention_mixer(h, s0, pos0, w_in, gn_g, w_out):
    B, L, _ = h.shape
    p = h @ w_in
    q = p[..., :RET_QW].reshape(B, L, RET_HEADS, RET_DK)
    k = p[..., RET_QW:2 * RET_QW].reshape(B, L, RET_HEADS, RET_DK)
    v = p[..., 2 * RET_QW:2 * RET_QW + RET_VW].reshape(B, L, RET_HEADS, RET_DV).astype(F32)
    gate = p[..., 2 * RET_QW + RET_VW:]
    q = _rotary(q, pos0)
    k = _rotary(k, pos0) * (RET_DK ** -0.5)
    o, s = _retention_chunked(q, k, v, s0.astype(F32))
    mu = o.mean(-1, keepdims=True)
    var = jnp.square(o - mu).mean(-1, keepdims=True)
    o = (o - mu) * lax.rsqrt(var + LN_EPS) * gn_g.astype(F32)
    o = o.reshape(B, L, RET_VW).astype(h.dtype) * jax.nn.silu(gate)
    return o @ w_out, s.astype(s0.dtype)

def _causal_conv(x, buf, w):
    L = x.shape[1]
    xp = jnp.concatenate([buf.astype(x.dtype), x], axis=1)
    y = xp[:, 0:L] * w[0]
    for t in range(1, DN_CONV_W):
        y = y + xp[:, t:t + L] * w[t]
    return y, xp[:, L:]

def _gated_delta_chunked(q, k, v, g, beta, s0):
    L = q.shape[1]
    c = min(DN_CHUNK, L)
    n = L // c
    incl = jnp.tril(jnp.ones((c, c), dtype=bool))
    strict = jnp.tril(jnp.ones((c, c), dtype=bool), -1)
    eye = jnp.eye(c, dtype=F32)

    def step(s, xs):
        qi, ki, vi, gi, bi = xs
        G = jnp.cumsum(gi, axis=-1)
        decay = jnp.exp(jnp.where(incl, G[..., :, None] - G[..., None, :], -jnp.inf))
        kb = ki * bi[..., None]
        a = jnp.where(strict, jnp.einsum('bhid,bhjd->bhij', kb, ki) * decay, 0.0)
        rhs = jnp.concatenate([vi * bi[..., None], kb * jnp.exp(G)[..., None]], axis=-1)
        sol = lax.linalg.triangular_solve(eye + a, rhs, left_side=True, lower=True,
                                          unit_diagonal=True)
        u = sol[..., :DN_DV] - sol[..., DN_DV:] @ s
        att = jnp.einsum('bhid,bhjd->bhij', qi, ki) * decay
        o = (qi * jnp.exp(G)[..., None]) @ s + att @ u
        g_last = G[..., -1:]
        s = (s * jnp.exp(g_last)[..., None]
             + jnp.einsum('bhjd,bhjv->bhdv', ki * jnp.exp(g_last - G)[..., None], u))
        return s, o

    xs = (_to_chunks(q, n, c), _to_chunks(k, n, c), _to_chunks(v, n, c),
          _to_chunks(g, n, c), _to_chunks(beta, n, c))
    s, o = lax.scan(step, s0, xs)
    return _from_chunks(o), s

def _deltanet_mixer(h, s0, buf, w_in, conv_w, a_log, dt_bias, norm_g, w_out):
    B, L, _ = h.shape
    p = h @ w_in
    qkv, buf_new = _causal_conv(p[..., :DN_CONV_CH], buf, conv_w)
    qkv = jax.nn.silu(qkv).astype(F32)
    z = p[..., DN_CONV_CH:DN_CONV_CH + DN_VW]
    a = p[..., DN_CONV_CH + DN_VW:DN_CONV_CH + DN_VW + DN_V_HEADS].astype(F32)
    b = p[..., DN_CONV_CH + DN_VW + DN_V_HEADS:].astype(F32)
    rep = DN_V_HEADS // DN_QK_HEADS
    q = _l2norm(qkv[..., :DN_QW].reshape(B, L, DN_QK_HEADS, DN_DK))
    k = _l2norm(qkv[..., DN_QW:2 * DN_QW].reshape(B, L, DN_QK_HEADS, DN_DK))
    q = jnp.repeat(q, rep, axis=2) * (DN_DK ** -0.5)
    k = jnp.repeat(k, rep, axis=2)
    v = qkv[..., 2 * DN_QW:].reshape(B, L, DN_V_HEADS, DN_DV)
    g = -jnp.exp(a_log.astype(F32)) * jax.nn.softplus(a + dt_bias.astype(F32))
    beta = jax.nn.sigmoid(b)
    o, s = _gated_delta_chunked(q, k, v, g, beta, s0.astype(F32))
    o = _rms_norm(o, norm_g) * jax.nn.silu(z.astype(F32).reshape(B, L, DN_V_HEADS, DN_DV))
    return o.reshape(B, L, DN_VW).astype(h.dtype) @ w_out, s.astype(s0.dtype), buf_new.astype(buf.dtype)

def _moe(h, w_router, b_router, w_gu, w_down):
    B, L, D = h.shape
    t = h.reshape(B * L, D)
    probs = jax.nn.softmax((t @ w_router).astype(F32), axis=-1)
    sel = probs + b_router.astype(F32)
    grp_score = lax.top_k(sel.reshape(-1, N_GROUPS, EXPERTS_PER_GROUP), GROUP_SCORE_K)[0].sum(-1)
    gsel = jnp.argmax(grp_score, axis=-1)
    in_grp = (jnp.arange(N_EXPERTS) // EXPERTS_PER_GROUP)[None, :] == gsel[:, None]
    _, eidx = lax.top_k(jnp.where(in_grp, sel, -jnp.inf), TOP_K)
    w = jnp.take_along_axis(probs, eidx, axis=-1)
    w = w / w.sum(-1, keepdims=True)
    gates = jnp.sum(jax.nn.one_hot(eidx, N_EXPERTS, dtype=F32) * w[..., None], axis=1)
    gu = jnp.einsum('td,edf->tef', t, w_gu)
    act = jax.nn.silu(gu[..., :D_EXPERT]) * gu[..., D_EXPERT:]
    act = act * gates.astype(act.dtype)[..., None]
    y = jnp.einsum('tef,efd->td', act, w_down)
    return y.reshape(B, L, D)

def _trunk(x, c, pos0, s_ret, s_dn, s_conv, w_ada, b_ada, ln_g, ln_b, ret_w_in, ret_gn_g, ret_w_out,
           dn_w_in, dn_conv_w, dn_a_log, dn_dt_bias, dn_norm_g, dn_w_out, router_w, router_b,
           moe_w_gu, moe_w_down):
    B = x.shape[0]
    new_ret, new_dn, new_conv = [], [], []
    cs = jax.nn.silu(c)
    for i in range(DEPTH):
        mod = (cs @ w_ada[i] + b_ada[i]).reshape(B, N_MOD, 1, D_MODEL)
        shift_m, scale_m, gate_m, shift_f, scale_f, gate_f = (mod[:, j] for j in range(N_MOD))
        h = x * (1.0 + scale_m) + shift_m
        j = i // N_MIXERS
        if i % N_MIXERS == 0:
            y, s = _retention_mixer(h, s_ret[j], pos0, ret_w_in[j], ret_gn_g[j], ret_w_out[j])
            new_ret.append(s)
        else:
            y, s, buf = _deltanet_mixer(h, s_dn[j], s_conv[j], dn_w_in[j], dn_conv_w[j], dn_a_log[j],
                                        dn_dt_bias[j], dn_norm_g[j], dn_w_out[j])
            new_dn.append(s)
            new_conv.append(buf)
        x = _layer_norm(ALPHA * x + (1.0 + gate_m) * y, ln_g[i, 0], ln_b[i, 0])
        h = x * (1.0 + scale_f) + shift_f
        y = _moe(h, router_w, router_b, moe_w_gu[i], moe_w_down[i])
        x = _layer_norm(ALPHA * x + (1.0 + gate_f) * y, ln_g[i, 1], ln_b[i, 1])
    return x, jnp.stack(new_ret), jnp.stack(new_dn), jnp.stack(new_conv)

def setup_inputs(seed: int = 0) -> dict:
    key = jax.random.key(seed)
    ks = jax.random.split(key, 32)

    def nrm(k, shape, scale):
        return jax.random.normal(k, shape, F32) * scale

    ret_cols = jnp.concatenate([jnp.ones((2 * RET_QW,), F32), jnp.full((RET_VW,), BETA_INIT, F32),
                                jnp.ones((RET_VW,), F32)])
    dn_cols = jnp.concatenate([jnp.ones((2 * DN_QW,), F32), jnp.full((DN_VW,), BETA_INIT, F32),
                               jnp.ones((DN_VW + 2 * DN_V_HEADS,), F32)])
    dt = jnp.exp(jax.random.uniform(ks[17], (N_DN_LAYERS, DN_V_HEADS), F32,
                                    jnp.log(1e-3), jnp.log(1e-1)))
    return {
        "x_prompt": nrm(ks[0], (BATCH, SEQ, D_MODEL), 1.0),
        "x_sample": nrm(ks[1], (DEC_BATCH, DEC_SEQ, D_MODEL), 1.0),
        "state_ret": nrm(ks[2], (N_RET_LAYERS, DEC_BATCH, RET_HEADS, RET_DK, RET_DV), 0.1),
        "state_dn": nrm(ks[3], (N_DN_LAYERS, DEC_BATCH, DN_V_HEADS, DN_DK, DN_DV), 0.1),
        "state_conv": nrm(ks[4], (N_DN_LAYERS, DEC_BATCH, DN_CONV_W - 1, DN_CONV_CH), 1.0),
        "c_prompt": nrm(ks[5], (BATCH, D_MODEL), 1.0),
        "c_sample": nrm(ks[6], (DEC_BATCH, D_MODEL), 1.0),
        "w_ada": nrm(ks[7], (DEPTH, D_MODEL, N_MOD * D_MODEL), 0.1 * D_MODEL ** -0.5),
        "b_ada": nrm(ks[8], (DEPTH, N_MOD * D_MODEL), 0.01),
        "ln_g": 1.0 + nrm(ks[9], (DEPTH, 2, D_MODEL), 0.02),
        "ln_b": nrm(ks[10], (DEPTH, 2, D_MODEL), 0.02),
        "ret_w_in": nrm(ks[11], (N_RET_LAYERS, D_MODEL, RET_IN), D_MODEL ** -0.5) * ret_cols,
        "ret_gn_g": 1.0 + nrm(ks[12], (N_RET_LAYERS, RET_DV), 0.02),
        "ret_w_out": nrm(ks[13], (N_RET_LAYERS, RET_VW, D_MODEL), BETA_INIT * RET_VW ** -0.5),
        "dn_w_in": nrm(ks[14], (N_DN_LAYERS, D_MODEL, DN_IN), D_MODEL ** -0.5) * dn_cols,
        "dn_conv_w": nrm(ks[15], (N_DN_LAYERS, DN_CONV_W, DN_CONV_CH), DN_CONV_W ** -0.5),
        "dn_a_log": jnp.log(jax.random.uniform(ks[16], (N_DN_LAYERS, DN_V_HEADS), F32, 1.0, 16.0)),
        "dn_dt_bias": dt + jnp.log(-jnp.expm1(-dt)),
        "dn_norm_g": 1.0 + nrm(ks[18], (N_DN_LAYERS, DN_DV), 0.02),
        "dn_w_out": nrm(ks[19], (N_DN_LAYERS, DN_VW, D_MODEL), BETA_INIT * DN_VW ** -0.5),
        "router_w": nrm(ks[20], (D_MODEL, N_EXPERTS), D_MODEL ** -0.5),
        "router_b": nrm(ks[21], (N_EXPERTS,), 0.01),
        "moe_w_gu": nrm(ks[22], (DEPTH, N_EXPERTS, D_MODEL, 2 * D_EXPERT), D_MODEL ** -0.5),
        "moe_w_down": nrm(ks[23], (DEPTH, N_EXPERTS, D_EXPERT, D_MODEL), BETA_INIT * D_EXPERT ** -0.5),
    }

def reference(x_prompt, x_sample, state_ret, state_dn, state_conv, c_prompt, c_sample, w_ada, b_ada,
              ln_g, ln_b, ret_w_in, ret_gn_g, ret_w_out, dn_w_in, dn_conv_w, dn_a_log, dn_dt_bias,
              dn_norm_g, dn_w_out, router_w, router_b, moe_w_gu, moe_w_down):
    b_p = x_prompt.shape[0]
    zr = jnp.zeros((N_RET_LAYERS, b_p) + state_ret.shape[2:], state_ret.dtype)
    zd = jnp.zeros((N_DN_LAYERS, b_p) + state_dn.shape[2:], state_dn.dtype)
    zc = jnp.zeros((N_DN_LAYERS, b_p) + state_conv.shape[2:], state_conv.dtype)
    y_prompt, ret_p, dn_p, conv_p = _trunk(
        x_prompt, c_prompt, 0, zr, zd, zc, w_ada, b_ada, ln_g, ln_b, ret_w_in, ret_gn_g, ret_w_out,
        dn_w_in, dn_conv_w, dn_a_log, dn_dt_bias, dn_norm_g, dn_w_out, router_w, router_b,
        moe_w_gu, moe_w_down)
    y_sample, ret_s, dn_s, conv_s = _trunk(
        x_sample, c_sample, PAST_LEN, state_ret, state_dn, state_conv, w_ada, b_ada, ln_g, ln_b,
        ret_w_in, ret_gn_g, ret_w_out, dn_w_in, dn_conv_w, dn_a_log, dn_dt_bias, dn_norm_g, dn_w_out,
        router_w, router_b, moe_w_gu, moe_w_down)
    return (y_prompt, y_sample, ret_p, ret_s, dn_p, dn_s, conv_p, conv_s)


_drawn_inputs = setup_inputs


def setup_inputs(seed=0):
    import zlib

    import numpy as np

    out = dict(_drawn_inputs(seed))
    spreads = {}
    factors = {'dn_norm_g': 5.232}
    for name, (base, spread) in spreads.items():
        noise = np.random.default_rng([zlib.crc32(name.encode()), seed]).standard_normal(out[name].shape)
        drawn = base * np.exp(spread * noise) if base else spread * noise
        out[name] = __import__('jax').numpy.asarray(drawn.astype(out[name].dtype))
    for name, factor in factors.items():
        out[name] = (out[name] * factor).astype(out[name].dtype)
    return out
```

```python
from contextlib import ExitStack

import numpy as np

import concourse.bass as bass
from concourse import mybir

F32 = mybir.dt.float32
I32 = mybir.dt.int32
U32 = mybir.dt.uint32
ALU = mybir.AluOpType
ACT = mybir.ActivationFunctionType
AX = mybir.AxisListType

P = 128
D = 1024
KD = D // P
SEQ, DECB, DECL = 512, 8, 4
NPT = SEQ // P
NS = DECB * DECL
NTOK = SEQ + NS
NT = NPT + 1
NMOD = 6
MODW = NMOD * D
W = 512
HEADS = 4
DK, DV = 256, 512
NE = 16
DE = 256
RING = 3
ALPHA = float((2.0 * 2) ** 0.25)
LN_EPS = 1e-5
RMS_EPS = 1e-6
MAXT = (2 * NTOK) // P + NE
MINT = (2 * NTOK) // P


def rows(t):
    return P if t < NPT else NS


def tok(t):
    return slice(P * t, P * t + rows(t))


class Chain:

    def __init__(self, eng, sem):
        self.eng, self.sem, self.n = eng, sem, 0

    def mark(self, ins):
        self.n += 1
        ins.then_inc(self.sem, 1)
        return self.n

    def __call__(self, ins):
        self.mark(ins)
        self.eng.wait_ge(self.sem, self.n)


class Core:

    def __init__(self, nc, ctx, dram):
        self.nc, self.ctx, self.dram = nc, ctx, dram
        self.ident = self.sb(ctx, "ident", [P, P])
        self.ones = self.sb(ctx, "ones", [P, P])
        self.eps = self.sb(ctx, "eps", [P, 4])
        self.hT = self.sb(ctx, "hT", [P, KD, NTOK])
        self.ring = self.sb(ctx, "ring", [P, RING, KD, W])
        self.ps = [ctx.enter_context(nc.psum_tensor(f"bank{i}", [P, W], F32)) for i in range(8)]
        self.landed = [ctx.enter_context(nc.semaphore(f"weights_landed{s}")) for s in range(RING)]
        self.ada_done = ctx.enter_context(nc.semaphore("ada_done"))
        self.proj_done = [ctx.enter_context(nc.semaphore(f"proj_done{l}")) for l in range(2)]
        self.blocks = [((self.ada_done, w + 1), 1) for w in range(2 * MODW // W)]
        self.base = [None, None]
        for l in range(2):
            self.base[l] = len(self.blocks)
            for j, pieces in enumerate(dram["mixer_blocks"][l]):
                n = NT * (j + 1) if l == 0 else 21 * (j // 3) + (8, 16, 21)[j % 3]
                self.blocks.append(((self.proj_done[l], n) if j < 12 else None, pieces))
        self.next = [b for b in self.base]

    def sb(self, ctx, name, shape, dt=F32):
        return ctx.enter_context(self.nc.sbuf_tensor(name, shape, dt))

    def arrival(self, w):
        n = sum(x if isinstance(x, int) else len(x) for _, x in self.blocks[w % RING:w + 1:RING])
        return self.landed[w % RING], 16 * n

    def mixer_weights(self, sp, l, count=1):
        for _ in range(count):
            w = self.next[l]
            free = self.blocks[w - RING][0]
            if free:
                sp.wait_ge(*free)
            for chunks, cols, src in self.blocks[w][1]:
                sp.dma_start(self.ring[:, w % RING, chunks, cols], src).then_inc(self.landed[w % RING], 16)
            self.next[l] += 1


class Stage:

    def __init__(self, core, name):
        self.core, self.name, self.sems, self.ctx = core, name, [], ExitStack()

    def __enter__(self):
        return self

    def sem(self, name):
        s = self.core.nc.alloc_semaphore(f"{self.name}_{name}")
        self.sems.append(s)
        return s

    def pool_sem(self, name):
        return self.core.nc.alloc_semaphore(f"{self.name}_{name}")

    def sb(self, name, shape, dt=F32):
        return self.core.sb(self.ctx, f"{self.name}_{name}", shape, dt)

    def __exit__(self, *exc):
        if exc[0] is None:
            nc = self.core.nc
            with nc.Block() as block:
                @block.gpsimd
                def _(pool):
                    for s in self.sems:
                        pool.sem_clear(s)
            for s in self.sems:
                nc.release_semaphore(s)
            self.ctx.close()
        return False


def setup_and_modulation(core):
    nc, d = core.nc, core.dram
    with Stage(core, "ada") as st:
        NC = 1 + DECB
        c_rows = st.sb("c_rows", [NC, D])
        cT = st.sb("cT", [P, KD, 32])
        parts = st.sb("parts", [P, RING, W])
        fold = st.sb("fold", [P, NC])
        mod = st.sb("mod", [NC, 2 * MODW])
        consts_in, c_in, bias_in = st.sem("consts_in"), st.sem("c_in"), st.sem("bias_in")
        zeroed, c_silu, c_turned, cT_ready = st.sem("zeroed"), st.sem("c_silu"), st.sem("c_turned"), st.sem("cT_ready")
        parts_kept, folded, block_kept = st.sem("parts_kept"), st.sem("folded"), st.sem("block_kept")
        mod_out = st.sem("mod_out")
        NB = 2 * MODW // W
        w_ada = [d["w_ada"][l].rearrange("(k p) n -> p k n", p=P) for l in range(2)]
        with nc.Block() as block:
            @block.sync
            def _(sp):
                sp.dma_start(core.ident[:, :], d["c_ident"]).then_inc(consts_in, 16)
                sp.dma_start(fold[:, :], d["c_fold"]).then_inc(consts_in, 16)
                sp.dma_start(core.eps[:, :], d["c_eps"]).then_inc(consts_in, 16)
                sp.dma_start(c_rows[0:1, :], d["c_prompt"]).then_inc(c_in, 16)
                sp.dma_start(c_rows[1:NC, :], d["c_sample"]).then_inc(c_in, 16)
                for l in range(2):
                    sp.dma_start(mod[:, l * MODW:(l + 1) * MODW],
                                 d["b_ada"][l:l + 1, :].broadcast_to([NC, MODW])).then_inc(bias_in, 16)
                for s in range(RING):
                    sp.dma_start(core.ring[:, s], w_ada[0][:, :, s * W:(s + 1) * W]).then_inc(core.landed[s], 16)
                per = MODW // W // RING
                for l in range(2):
                    with sp.Fori(1 - l, per) as i:
                        for s in range(RING):
                            sp.wait_ge(core.ada_done, i * RING + (l * per * RING + s - RING + 1))
                            sp.dma_start(core.ring[:, s], w_ada[l][:, :, bass.ds((i * RING + s) * W, W)]
                                         ).then_inc(core.landed[s], 16)
                core.mixer_weights(sp, 0, RING)
                for l in range(2):
                    sp.wait_ge(block_kept, NB // 2 * (l + 1) + RING)
                    sp.dma_start(d["mod"][:, l * MODW:(l + 1) * MODW],
                                 mod[:, l * MODW:(l + 1) * MODW]).then_inc(mod_out, 16)
                sp.wait_ge(mod_out, 32)
                sp.wait_ge(consts_in, 48)

            @block.gpsimd
            def _(pool):
                pool.memset(core.ones[:, :], 1.0).then_inc(zeroed, 1)
                pool.memset(cT[:, :, :], 0.0).then_inc(zeroed, 1)

            @block.scalar
            def _(act):
                act.wait_ge(c_in, 32)
                act.activation(c_rows[:, :], c_rows[:, :], ACT.Silu).then_inc(c_silu, 1)
                act.wait_ge(zeroed, 2)
                act.wait_ge(c_turned, 1)
                act.activation(cT[:, :, 0:NC], core.ps[7][:, 0:KD * NC].rearrange("p (k m) -> p k m", k=KD),
                               ACT.Copy).then_inc(cT_ready, 1)
                with act.Fori(0, NB // RING) as i:
                    for s in range(RING):
                        act.wait_ge(core.ada_done, i * RING + (s + 1))
                        act.activation(parts[:, s, :], core.ps[s][:, :], ACT.Copy).then_inc(parts_kept, 1)

            @block.tensor
            def _(pe):
                pe.wait_ge(consts_in, 48)
                pe.wait_ge(c_silu, 1)
                for k in range(KD):
                    last = pe.transpose(core.ps[7][:, k * NC:(k + 1) * NC], c_rows[:, k * P:(k + 1) * P],
                                        core.ident[0:NC, 0:NC])
                last.then_inc(c_turned, 1)
                pe.wait_ge(cT_ready, 1)

                def products(i, s):
                    pe.wait_ge(core.landed[s], i * 16 + 16)
                    for k in range(KD):
                        j = k % 4
                        last = pe.matmul(core.ps[s][32 * j:32 * j + 32, :], cT[:, k, :], core.ring[:, s, k, :],
                                         start=(k < 4), stop=(k >= 4), skip_group_check=True)
                    last.then_inc(core.ada_done, 1)

                def fold_up(i, s):
                    pe.wait_ge(parts_kept, i * RING + (s + 1))
                    pe.wait_ge(block_kept, i * RING + RING)
                    pe.matmul(core.ps[RING + s][0:NC, :], fold[:, :], parts[:, s, :],
                              start=True, stop=True).then_inc(folded, 1)

                with pe.Fori(0, NB // RING) as i:
                    products(i, 0)
                    products(i, 1)
                    fold_up(i, 0)
                    products(i, 2)
                    fold_up(i, 1)
                    fold_up(i, 2)

            @block.vector
            def _(dve):
                dve.sem_inc(block_kept, RING)
                dve.wait_ge(bias_in, 32)
                with dve.Fori(0, NB // RING) as i:
                    for s in range(RING):
                        dve.wait_ge(folded, i * RING + (s + 1))
                        cols = bass.ds((i * RING + s) * W, W)
                        dve.tensor_tensor(mod[:, cols], core.ps[RING + s][0:NC, :], mod[:, cols],
                                          ALU.add).then_inc(block_kept, 1)


def vectors_in(sp, d, l, part, to, sem):
    cols = slice(l * MODW + part * D, l * MODW + (part + 1) * D)
    sp.dma_start(to[:, 0, :], d["mod"][0:1, cols].broadcast_to([P, D])).then_inc(sem, 16)
    sp.dma_start(to[0:NS, 1, :], d["mod"][1:1 + DECB, cols].unsqueeze(1).broadcast_to([DECB, DECL, D])
                 ).then_inc(sem, 16)


def turn_tile(pe, core, src, t, banks):
    n = rows(t)
    for k in range(KD):
        last = pe.transpose(core.ps[banks[k // 4]][:, (k % 4) * n:(k % 4 + 1) * n],
                            src[0:n, k * P:(k + 1) * P], core.ident[0:n, 0:n])
    return last


def keep_turned(act, core, t, banks, done, dst=None):
    n = rows(t)
    for half in range(2):
        to = core.hT[:, 4 * half:4 * half + 4, tok(t)] if dst is None else dst[:, 4 * half:4 * half + 4, 0:n]
        act.activation(to, core.ps[banks[half]][:, 0:4 * n].rearrange("p (k n) -> p k n", k=4),
                       ACT.Copy).then_inc(done, 1)


def first_features(core):
    nc, d = core.nc, core.dram
    with Stage(core, "in") as st:
        x = st.sb("x", [P, NT, D])
        shift, scale = st.sb("shift", [P, 2, D]), st.sb("scale", [P, 2, D])
        x_in, vec_in, steps, h_done, turned, kept = (st.sem(n) for n in (
            "x_in", "vec_in", "steps", "h_done", "turned", "kept"))
        with nc.Block() as block:
            @block.sync
            def _(sp):
                vectors_in(sp, d, 0, 0, shift, vec_in)
                vectors_in(sp, d, 0, 1, scale, vec_in)
                for t in range(NT):
                    sp.dma_start(x[0:rows(t), t, :], d["x0"](t)).then_inc(x_in, 16)

            @block.vector
            def _(dve):
                chain = Chain(dve, steps)
                dve.wait_ge(vec_in, 64)
                dve.wait_ge(x_in, 16 * NT)
                for t in range(NT):
                    n, v = rows(t), t // NPT
                    chain(dve.scalar_tensor_tensor(x[0:n, t, :], scale[0:n, v, :], 1.0, x[0:n, t, :],
                                                   ALU.add, ALU.mult))
                    dve.tensor_tensor(x[0:n, t, :], x[0:n, t, :], shift[0:n, v, :], ALU.add).then_inc(h_done, 1)

            @block.tensor
            def _(pe):
                for t in range(NT):
                    pe.wait_ge(h_done, t + 1)
                    if t >= 2:
                        pe.wait_ge(kept, 2 * (t - 1))
                    turn_tile(pe, core, x[:, t, :], t, (2 * (t % 2), 2 * (t % 2) + 1)).then_inc(turned, 1)

            @block.scalar
            def _(act):
                for t in range(NT):
                    act.wait_ge(turned, t + 1)
                    keep_turned(act, core, t, (2 * (t % 2), 2 * (t % 2) + 1), kept)


def retention(core):
    nc, d = core.nc, core.dram
    ps = core.ps
    H = HEADS
    UNITS = 3 * NT
    with Stage(core, "ret") as st:
        qk = st.sb("qk", [P, NT, W])
        turned = st.sb("turned", [P, 4, P])
        v, gate = st.sb("v", [P, 2, NT, W]), st.sb("gate", [P, 2, NT, W])
        qkT = st.sb("qkT", [P, 4, NTOK])
        qdT = st.sb("qdT", [P, 2, NTOK])
        kd = st.sb("kd", [P, NPT, DK])
        kds = st.sb("kds", [NS, 2, DK])
        qds = st.sb("qds", [P, 2, DECB, NS])
        att, att_s = st.sb("att", [P, NPT, P]), st.sb("att_s", [NS, NS])
        S = st.sb("S", [P, 2, DV])
        Ss = st.sb("Ss", [P, 2, 2, DV])
        cos, sin = st.sb("cos", [P, NT, P]), st.sb("sin", [P, NT, P])
        dec, dec_s = st.sb("dec", [P, H, P]), st.sb("dec_s", [NS, H, NS])
        qdec = st.sb("qdec", [P, H, P + NS])
        kdec = st.sb("kdec", [P, H])
        kdec_s = st.sb("kdec_s", [NS, H, DECB])
        sdec = st.sb("sdec", [P, 2, H])
        seqmask = st.sb("seqmask", [P, DECB, NS])
        gn = st.sb("gn", [P, DV])
        stats, mom = st.sb("stats", [P, 2, 6]), st.sb("mom", [P, 2, 2])
        var, rstd = st.sb("var", [P, 2, 1]), st.sb("rstd", [P, 2, 1])
        og = st.sb("og", [P, 2, DV])
        oT = core.oT
        s = {n: st.sem(n) for n in (
            "consts", "vg_taken", "qk_taken", "rot", "zeroed", "zeros_out", "kds_done", "dsteps", "psteps", "qkT_turned", "qkT_kept", "qdT_done", "kd_done",
            "qds_done", "att_ps", "att_done", "o_ps", "o_done", "st_ps", "st_done", "ss_in0", "ss_in1", "ss_out0", "ss_out1",
            "ss_ps", "ss_done", "moments", "rstd_done", "gated", "oT_ps", "oT_kept", "s_out", "gate_done",
            "gn_in")}
        proj = core.proj_done[0]

        def taken(u):
            h, r = u // UNITS, u % UNITS
            if r < 2 * NT:
                return s["vg_taken"], 2 * NT * h + r + 1
            return s["qk_taken"], NT * h + r - 2 * NT + 1

        def o_unit(h, t):
            return NT * h + t

        STEPS = {0: [("turn", 0), ("turn", 1)], 1: [("turn", 2), ("turn", 3)], 2: [("turn", 4), ("scores", 0)],
                 3: [("chunk", 0)], 4: [("chunk", 1), ("norm", 0)], 5: [("chunk", 2), ("norm", 1)],
                 6: [("out", 0), ("chunk", 3), ("norm", 2)], 7: [("out", 1), ("norm", 3), ("seqs", 0)],
                 8: [("seqs", 1), ("out", 2)], 9: [("seqs", 2)], 10: [("seqs", 3), ("out", 3)],
                 11: [("norm", 4)], 12: [("out", 4)]}

        def program(project, step):
            for h in range(H + 1):
                for u in range(UNITS):
                    if h < H:
                        project(h, u // NT, u % NT, UNITS * h + u)
                    if h > 0:
                        for what, i in STEPS.get(u, ()):
                            step(what, h - 1, i)

        def nothing(*_):
            pass

        with nc.Block() as block:
            @block.sync
            def _(sp):
                for to, name in ((cos, "c_cos"), (sin, "c_sin"), (dec, "c_dec"), (qdec, "c_qdec"), (kdec, "c_kdec"),
                                 (sdec, "c_sdec"), (seqmask, "c_seqmask")):
                    sp.dma_start(to[:], d[name]).then_inc(s["consts"], 16)
                sp.dma_start(dec_s[:], d["c_dec_s"]).then_inc(s["consts"], 16)
                sp.dma_start(kdec_s[:], d["c_kdec_s"]).then_inc(s["consts"], 16)
                sp.dma_start(gn[:], d["ret_gn_g"].broadcast_to([P, DV])).then_inc(s["consts"], 16)
                sp.wait_ge(s["zeroed"], 1)
                for i in range(MINT, MAXT):
                    sp.dma_start(d["y_rows"][P * i:P * (i + 1), :], og[:].rearrange("p a n -> p (a n)")
                                 ).then_inc(s["zeros_out"], 16)
                for i in range(MAXT):
                    sp.dma_start(d["rows"][P * i:P * (i + 1), :], og[:].rearrange("p a n -> p (a n)")
                                 ).then_inc(s["zeros_out"], 16)

                def project(h, b, t, u):
                    if t == 0 and (h, b) != (0, 0):
                        core.mixer_weights(sp, 0)

                def state_in(h, b):
                    n = DECB * h + b
                    if n >= 2:
                        sp.wait_ge(s[f"ss_out{n % 2}"], 16 * (n // 2))
                    sp.dma_start(Ss[:, n % 2], d["state_ret"][0, b, h].rearrange("(a p) v -> p a v", p=P)
                                 ).then_inc(s[f"ss_in{n % 2}"], 16)

                def step(what, h, i):
                    if what == "chunk" and i == NPT - 1:
                        sp.wait_ge(s["st_done"], 2 * NPT * (h + 1))
                        sp.dma_start(d["ret_p"][0, 0, h].rearrange("(a p) v -> p a v", p=P), S[:]
                                     ).then_inc(s["s_out"], 16)
                    if what == "turn" and i == 0 and h == 0:
                        state_in(0, 0)
                        state_in(0, 1)
                    if what == "seqs":
                        for b in (2 * i, 2 * i + 1):
                            n = DECB * h + b
                            sp.wait_ge(s["ss_done"], 2 * (n + 1))
                            sp.dma_start(d["ret_s"][0, b, h].rearrange("(a p) v -> p a v", p=P), Ss[:, n % 2]
                                         ).then_inc(s[f"ss_out{n % 2}"], 16)
                            if n + 2 < DECB * H:
                                state_in((n + 2) // DECB, (n + 2) % DECB)

                program(project, step)
                core.mixer_weights(sp, 0)
                sp.wait_ge(s["s_out"], 16 * H)
                for k in range(2):
                    sp.wait_ge(s[f"ss_out{k}"], 16 * H * DECB // 2)

            @block.tensor
            def _(pe):
                pe.wait_ge(s["consts"], 160)

                def project(h, b, t, u):
                    w = core.base[0] + 3 * h + b
                    if t == 0:
                        pe.wait_ge(*core.arrival(w))
                    if u >= 2:
                        pe.wait_ge(*taken(u - 2))
                    for k in range(KD):
                        last = pe.matmul(ps[u % 2][0:rows(t), :], core.hT[:, k, tok(t)], core.ring[:, w % RING, k, :],
                                         start=(k == 0), stop=(k == KD - 1))
                    last.then_inc(proj, 1)

                def step(what, h, i):
                    if what == "turn":
                        n, x = rows(i), NT * h + i
                        pe.wait_ge(s["rot"], x + 1)
                        if x >= 2:
                            pe.wait_ge(s["qkT_kept"], x - 1)
                        if i < 2 and h > 0:
                            pe.wait_ge(s["ss_done"], 2 * DECB * h)
                        for c in range(4):
                            last = pe.transpose(ps[2 + x % 2][:, c * n:(c + 1) * n], qk[0:n, i, c * P:(c + 1) * P],
                                                core.ident[0:n, 0:n])
                        last.then_inc(s["qkT_turned"], 1)
                    if what == "scores":
                        pe.wait_ge(s["qkT_kept"], NT * (h + 1))
                        if h > 0:
                            pe.wait_ge(s["oT_kept"], NT * h)
                        for t in range(NT):
                            n = rows(t)
                            out = ps[4][:, t * P:(t + 1) * P] if t < NPT else ps[5][0:NS, 0:NS]
                            for a in range(2):
                                last = pe.matmul(out, qkT[:, 2 + a, tok(t)], qkT[:, a, tok(t)],
                                                 start=(a == 0), stop=(a == 1))
                        last.then_inc(s["att_ps"], 1)
                    if what == "chunk":
                        x = o_unit(h, i)
                        if i == 0:
                            pe.wait_ge(s["att_done"], 2 * (h + 1))
                            pe.wait_ge(s["kd_done"], NPT * (h + 1))
                            pe.wait_ge(s["qdT_done"], NT * (h + 1))
                        if x >= 2:
                            pe.wait_ge(s["o_done"], x - 1)
                        if i > 0:
                            pe.wait_ge(s["st_done"], 2 * (NPT * h + i))
                        o = ps[6 + x % 2]
                        last = pe.matmul(o[:, :], att[:, i, :], v[:, h % 2, i, :], start=True, stop=(i == 0))
                        if i > 0:
                            for a in range(2):
                                last = pe.matmul(o[:, :], qdT[:, a, tok(i)], S[:, a, :], start=False, stop=(a == 1))
                        last.then_inc(s["o_ps"], 1)
                        for a in range(2):
                            last = pe.matmul(ps[2 + a][:, :], kd[:, i, a * P:(a + 1) * P], v[:, h % 2, i, :],
                                             start=True, stop=True)
                        last.then_inc(s["st_ps"], 1)
                    if what == "seqs":
                        x = o_unit(h, NPT)
                        o = ps[6 + x % 2]
                        if i == 0:
                            pe.wait_ge(s["o_done"], x - 1)
                            pe.wait_ge(s["qds_done"], h + 1)
                            pe.wait_ge(s["st_done"], 2 * NPT * (h + 1))
                            pe.matmul(o[0:NS, :], att_s[:, :], v[0:NS, h % 2, NPT, :], start=True, stop=False)
                        for b in (2 * i, 2 * i + 1):
                            n = DECB * h + b
                            pe.wait_ge(s[f"ss_in{n % 2}"], 16 * (n // 2 + 1))
                            for a in range(2):
                                last = pe.matmul(o[0:NS, :], qds[:, a, b, :], Ss[:, n % 2, a, :],
                                                 start=False, stop=(b == DECB - 1 and a == 1))
                            if b == DECB - 1:
                                last.then_inc(s["o_ps"], 1)
                            if b > 0:
                                pe.wait_ge(s["ss_done"], 2 * n)
                            pe.wait_ge(s["kds_done"], n + 1)
                            for a in range(2):
                                last = pe.matmul(ps[2 + a][:, :], kds[:, n % 2, a * P:(a + 1) * P], v[0:NS, h % 2, NPT, :],
                                                 start=True, stop=True)
                            last.then_inc(s["ss_ps"], 1)
                    if what == "out":
                        x, n = o_unit(h, i), rows(i)
                        pe.wait_ge(s["gated"], x + 1)
                        if i == 0:
                            pe.wait_ge(s["att_done"], 2 * (h + 1))
                        if x >= 2:
                            pe.wait_ge(s["oT_kept"], x - 1)
                        for c in range(4):
                            last = pe.transpose(ps[4 + x % 2][:, c * n:(c + 1) * n], og[0:n, x % 2, c * P:(c + 1) * P],
                                                core.ident[0:n, 0:n])
                        last.then_inc(s["oT_ps"], 1)

                program(project, step)

            @block.scalar
            def _(act):
                def project(h, b, t, u):
                    if b == 2:
                        return
                    n = rows(t)
                    act.wait_ge(proj, u + 1)
                    if t == 0 and h >= 2:
                        act.wait_ge(s["gated"], NT * (h - 1))
                        act.wait_ge(s["ss_done"], 2 * DECB * (h - 1))
                    dst = (v, gate)[b]
                    act.activation(dst[0:n, h % 2, t, :], ps[u % 2][0:n, :], (ACT.Copy, ACT.Silu)[b]
                                   ).then_inc(s["vg_taken"], 1)

                def step(what, h, i):
                    n = rows(i)
                    if what == "turn":
                        x = NT * h + i
                        act.wait_ge(s["qkT_turned"], x + 1)
                        if i == 0 and h > 0:
                            act.wait_ge(s["att_ps"], h)
                        act.activation(qkT[:, :, tok(i)], ps[2 + x % 2][:, 0:4 * n].rearrange("p (c n) -> p c n", c=4),
                                       ACT.Copy).then_inc(s["qkT_kept"], 1)
                    if what == "out":
                        x = o_unit(h, i)
                        act.wait_ge(s["oT_ps"], x + 1)
                        act.activation(oT[:, 4 * h:4 * h + 4, tok(i)],
                                       ps[4 + x % 2][:, 0:4 * n].rearrange("p (c n) -> p c n", c=4),
                                       ACT.Copy).then_inc(s["oT_kept"], 1)

                program(project, step)

            @block.gpsimd
            def _(pool):
                chain = Chain(pool, s["psteps"])
                pool.memset(og[:], 0.0).then_inc(s["zeroed"], 1)
                pool.wait_ge(s["consts"], 160)

                def project(h, b, t, u):
                    if b == 1:
                        pool.wait_ge(*taken(u))
                        n = rows(t)
                        pool.tensor_tensor(gate[0:n, h % 2, t, :], gate[0:n, h % 2, t, :], gn[0:n, :],
                                           ALU.mult).then_inc(s["gate_done"], 1)

                def step(what, h, i):
                    if what == "turn":
                        pool.wait_ge(s["rot"], NT * h + i + 1)
                        if i == 0 and h > 0:
                            pool.wait_ge(s["ss_ps"], DECB * h)
                        if i < NPT:
                            pool.tensor_scalar(kd[:, i, :], qk[:, i, DK:2 * DK], kdec[:, h:h + 1], 1.0,
                                               ALU.mult, ALU.mult).then_inc(s["kd_done"], 1)
                    if what == "seqs":
                        for b in (2 * i, 2 * i + 1):
                            n = DECB * h + b
                            if n >= 2:
                                pool.wait_ge(s["ss_ps"], n - 1)
                            pool.tensor_scalar(kds[:, n % 2, :], qk[0:NS, NPT, DK:2 * DK], kdec_s[:, h, b:b + 1], 1.0,
                                               ALU.mult, ALU.mult).then_inc(s["kds_done"], 1)
                    if what == "norm":
                        x, n = o_unit(h, i), rows(i)
                        pool.wait_ge(s["moments"], x + 1)
                        chain(pool.tensor_scalar(var[0:n, x % 2, :], mom[0:n, x % 2, 1:2], LN_EPS, 1.0,
                                                 ALU.add, ALU.mult))
                        pool.tensor_tensor(rstd[0:n, x % 2, :], var[0:n, x % 2, :], core.eps[0:n, 3:4],
                                           ALU.pow).then_inc(s["rstd_done"], 1)

                program(project, step)

            @block.vector
            def _(dve):
                chain = Chain(dve, s["dsteps"])
                dve.wait_ge(s["consts"], 160)

                def project(h, b, t, u):
                    if b != 2:
                        return
                    n = rows(t)
                    x = NT * h + t
                    dve.wait_ge(proj, u + 1)
                    src = ps[u % 2][0:n, :].rearrange("p (g f) -> p g f", f=P)
                    bc = lambda tab: tab[0:n, t, :].unsqueeze(1).broadcast_to([n, 4, P])
                    if h > 0:
                        dve.wait_ge(s["qkT_turned"], x - NT + 1)
                        if t < NPT:
                            dve.wait_ge(s["kd_done"], NPT * (h - 1) + t + 1)
                        else:
                            dve.wait_ge(s["kds_done"], DECB * h)
                    chain.mark(dve.tensor_tensor(turned[0:n], src, bc(cos), ALU.mult))
                    A = turned[0:n].rearrange("p (s e) f -> p s e f", e=2)
                    X = src.rearrange("p (s e) f -> p s e f", e=2)
                    out = qk[0:n, t, :].rearrange("p (s e f) -> p s e f", e=2, f=P)
                    sines = sin[0:n, t, :].unsqueeze(1).broadcast_to([n, 2, P])
                    chain.mark(dve.tensor_tensor(out[:, :, 1, :], X[:, :, 0, :], sines, ALU.mult))
                    dve.tensor_tensor(out[:, :, 0, :], X[:, :, 1, :], sines, ALU.mult).then_inc(s["qk_taken"], 1)
                    dve.wait_ge(*taken(u))
                    dve.wait_ge(s["dsteps"], chain.n)
                    chain.mark(dve.tensor_tensor(out[:, :, 0, :], A[:, :, 0, :], out[:, :, 0, :], ALU.subtract))
                    dve.tensor_tensor(out[:, :, 1, :], A[:, :, 1, :], out[:, :, 1, :], ALU.add).then_inc(s["rot"], 1)
                    dve.wait_ge(s["rot"], x + 1)
                    dve.wait_ge(s["dsteps"], chain.n)

                def step(what, h, i):
                    n = rows(i)
                    if what == "turn":
                        x = NT * h + i
                        dve.wait_ge(s["qkT_kept"], x + 1)
                        if h > 0:
                            dve.wait_ge(s["o_ps"], NT * h)
                        lo = 0 if i < NPT else P
                        dve.tensor_tensor(qdT[:, :, tok(i)], qkT[:, 0:2, tok(i)],
                                          qdec[:, h, lo:lo + n].unsqueeze(1).broadcast_to([P, 2, n]),
                                          ALU.mult).then_inc(s["qdT_done"], 1)
                        if i == NPT:
                            dve.wait_ge(s["qdT_done"], x + 1)
                            for a in range(2):
                                last = dve.tensor_tensor(
                                    qds[:, a], qdT[:, a, tok(i)].unsqueeze(1).broadcast_to([P, DECB, n]),
                                    seqmask[:], ALU.mult)
                                if a == 0:
                                    chain.mark(last)
                            last.then_inc(s["qds_done"], 1)
                            dve.wait_ge(s["dsteps"], chain.n)
                    if what == "scores":
                        dve.wait_ge(s["att_ps"], h + 1)
                        dve.tensor_tensor(att[:], ps[4][:, :].rearrange("p (t n) -> p t n", t=NPT),
                                          dec[:, h, :].unsqueeze(1).broadcast_to([P, NPT, P]),
                                          ALU.mult).then_inc(s["att_done"], 1)
                        dve.tensor_tensor(att_s[:], ps[5][0:NS, 0:NS], dec_s[:, h, :], ALU.mult
                                          ).then_inc(s["att_done"], 1)
                    if what == "chunk" or (what == "seqs" and i == 3):
                        t = i if what == "chunk" else NPT
                        x, n = o_unit(h, t), rows(t)
                        dve.wait_ge(s["o_ps"], x + 1)
                        chain(dve.bn_stats(stats[0:n, x % 2, :], ps[6 + x % 2][0:n, :]))
                        if x >= 2:
                            dve.wait_ge(s["rstd_done"], x - 1)
                        dve.bn_aggr(mom[0:n, x % 2, :], stats[0:n, x % 2, :]).then_inc(s["moments"], 1)
                    if what == "chunk":
                        y = NPT * h + i
                        dve.wait_ge(s["st_ps"], y + 1)
                        if i == 0 and h > 0:
                            dve.wait_ge(s["s_out"], 16 * h)
                        if i > 0:
                            dve.wait_ge(s["st_done"], 2 * y)
                        for a in range(2):
                            if i == 0:
                                last = dve.tensor_copy(S[:, a, :], ps[2 + a][:, :])
                            else:
                                last = dve.scalar_tensor_tensor(S[:, a, :], S[:, a, :], sdec[:, 0, h:h + 1],
                                                                ps[2 + a][:, :], ALU.mult, ALU.add)
                            last.then_inc(s["st_done"], 1)
                    if what == "seqs":
                        for b in (2 * i, 2 * i + 1):
                            y = DECB * h + b
                            dve.wait_ge(s["ss_ps"], y + 1)
                            for a in range(2):
                                dve.scalar_tensor_tensor(Ss[:, y % 2, a, :], Ss[:, y % 2, a, :], sdec[:, 1, h:h + 1],
                                                         ps[2 + a][:, :], ALU.mult, ALU.add).then_inc(s["ss_done"], 1)
                    if what == "norm":
                        x, n = o_unit(h, i), rows(i)
                        dve.wait_ge(s["moments"], x + 1)
                        dve.wait_ge(s["gate_done"], x + 1)
                        if x >= 2:
                            dve.wait_ge(s["oT_ps"], x - 1)
                        if x == 0:
                            dve.wait_ge(s["zeros_out"], 16 * (2 * MAXT - MINT))
                        dve.scalar_tensor_tensor(og[0:n, x % 2, :], ps[6 + x % 2][0:n, :], mom[0:n, x % 2, 0:1],
                                                 gate[0:n, h % 2, i, :], ALU.subtract, ALU.mult
                                                 ).then_inc(s["o_done"], 1)
                        dve.wait_ge(s["rstd_done"], x + 1)
                        dve.wait_ge(s["o_done"], x + 1)
                        dve.tensor_scalar(og[0:n, x % 2, :], og[0:n, x % 2, :], rstd[0:n, x % 2, :], None,
                                          ALU.mult).then_inc(s["gated"], 1)

                program(project, step)


class Gates:

    def __init__(self, core, ctx):
        f = lambda name, *shape: core.sb(ctx, "dn_" + name, [P, *shape])
        self.g, self.G, self.beta = f("g", NT, 16), f("G", NT, 16), f("beta", NT, 16)
        self.eG, self.beG = f("eG", NT, 16), f("beG", NT, 16)
        self.kdec = f("kdec", NT, 16)
        self.egl, self.egls = f("egl", NPT, 16), f("egls", DECB, 16)
        self.conv = f("conv", 32, 28)


def delta_gates(core, t, masks):
    nc, d, ps = core.nc, core.dram, core.ps
    with Stage(core, "gates") as st:
        wab, ab = st.sb("wab", [P, KD, 32]), st.sb("ab", [P, NT, 32])
        dt, al, rowmask = st.sb("dt", [P, 16]), st.sb("al", [P, 16]), st.sb("rowmask", [P, NT])
        x, e = st.sb("x", [P, NT, 16]), st.sb("e", [P, NT, 16])
        gseq = st.sb("gseq", [NS, DECB, 16])
        own = st.sb("own", [NS, DECB])
        tri, tri_s, same = masks["incl"], masks["incl_s"], masks["same"]
        rows28 = st.sb("rows28", [28, 4096])
        s = {n: st.sem(n) for n in ("ins", "conv_in", "zeroed", "ab_done", "ab_kept", "x_done", "absd", "exped", "lned", "aled",
                                    "beta_done", "steps", "g_done", "sums_done", "G_kept", "dif_done", "out_done",
                                    "conv_ps", "conv_kept")}
        with nc.Block() as block:
            @block.sync
            def _(sp):
                sp.dma_start(wab[:], d["dn_w_in"][0, :, 6144:6176].rearrange("(k p) n -> p k n", p=P)).then_inc(s["ins"], 16)
                sp.dma_start(dt[:], d["dn_dt_bias"].broadcast_to([P, 16])).then_inc(s["ins"], 16)
                sp.dma_start(al[:], d["dn_a_log"].broadcast_to([P, 16])).then_inc(s["ins"], 16)
                sp.dma_start(rowmask[:], d["c_rowmask"]).then_inc(s["ins"], 16)
                sp.dma_start(own[:], d["c_own"]).then_inc(s["ins"], 16)
                for name, to in masks.items():
                    sp.dma_start(to[:], d["c_" + name]).then_inc(s["ins"], 16)
                sp.dma_start(rows28[0:4, :], d["dn_conv_w"][0]).then_inc(s["conv_in"], 16)
                sp.dma_start(rows28[4:28, :], d["state_conv"][0].rearrange("b r c -> (b r) c")).then_inc(s["conv_in"], 16)
            total = 16 * (5 + len(masks))

            @block.tensor
            def _(pe):
                pe.wait_ge(s["ins"], total)
                for i in range(NT):
                    for k in range(KD):
                        last = pe.matmul(ps[0][0:rows(i), i * 32:(i + 1) * 32], core.hT[:, k, tok(i)], wab[:, k, :],
                                         start=(k == 0), stop=(k == KD - 1))
                last.then_inc(s["ab_done"], 1)
                pe.wait_ge(s["conv_in"], 32)
                for c in range(32):
                    last = pe.transpose(ps[4 + c // 16][:, (c % 16) * 28:(c % 16 + 1) * 28], rows28[:, c * P:(c + 1) * P],
                                        core.ident[0:28, 0:28])
                last.then_inc(s["conv_ps"], 1)
                pe.wait_ge(s["g_done"], 2)
                for i in range(NT):
                    n = rows(i)
                    last = pe.matmul(ps[1][0:n, i * 16:(i + 1) * 16], (tri if i < NPT else tri_s)[0:n, 0:n], t.g[0:n, i, :],
                                     start=True, stop=True)
                last.then_inc(s["sums_done"], 1)
                for i in range(NT):
                    n = rows(i)
                    last = pe.matmul(ps[2][0:n, i * 16:(i + 1) * 16], core.ones[:, :] if i < NPT else same[:, :], t.g[0:n, i, :],
                                     start=True, stop=True)
                last.then_inc(s["sums_done"], 1)
                pe.matmul(ps[3][:, 0:P], core.ones[0:NS, :], gseq[:].rearrange("p b h -> p (b h)"),
                          start=True, stop=True).then_inc(s["sums_done"], 1)

            @block.scalar
            def _(act):
                act.wait_ge(s["ab_done"], 1)
                act.wait_ge(s["zeroed"], 1)
                act.activation(ab[:, 0:NPT, :], ps[0][:, 0:NPT * 32].rearrange("p (t n) -> p t n", n=32), ACT.Copy
                               ).then_inc(s["ab_kept"], 1)
                act.activation(ab[0:NS, NPT, :], ps[0][0:NS, NPT * 32:NT * 32], ACT.Copy).then_inc(s["ab_kept"], 1)
                act.wait_ge(s["x_done"], 1)
                act.activation(e[:], x[:], ACT.Abs).then_inc(s["absd"], 1)
                act.wait_ge(s["absd"], 1)
                act.activation(e[:], e[:], ACT.Exp, scale=-1.0).then_inc(s["exped"], 1)
                act.wait_ge(s["ins"], total)
                act.activation(al[:], al[:], ACT.Exp).then_inc(s["aled"], 1)
                act.wait_ge(s["exped"], 1)
                act.activation(e[:], e[:], ACT.Ln, bias=1.0).then_inc(s["lned"], 1)
                act.activation(t.beta[:], ab[:, :, 16:32], ACT.Sigmoid).then_inc(s["beta_done"], 1)
                act.wait_ge(s["conv_ps"], 1)
                for i in range(2):
                    act.activation(t.conv[:, 16 * i:16 * i + 16, :], ps[4 + i][:, 0:448].rearrange("p (c n) -> p c n", n=28),
                                   ACT.Copy).then_inc(s["conv_kept"], 1)
                act.wait_ge(s["dif_done"], 1)
                act.activation(t.eG[:], t.G[:], ACT.Exp).then_inc(s["out_done"], 1)
                act.activation(t.kdec[:], t.kdec[:], ACT.Exp).then_inc(s["out_done"], 1)
                act.activation(t.egl[:], ps[2][:, 0:NPT * 16].rearrange("p (t h) -> p t h", h=16), ACT.Exp
                               ).then_inc(s["out_done"], 1)
                act.wait_ge(s["sums_done"], 3)
                act.activation(t.egls[:], ps[3][:, 0:P].rearrange("p (b h) -> p b h", h=16), ACT.Exp).then_inc(s["out_done"], 1)

            @block.vector
            def _(dve):
                chain = Chain(dve, s["steps"])
                dve.memset(ab[:], 0.0).then_inc(s["zeroed"], 1)
                chain.mark(dve.memset(t.G[:], 0.0))
                chain(dve.memset(t.kdec[:], 0.0))
                dve.wait_ge(s["ins"], total)
                dve.wait_ge(s["ab_kept"], 2)
                dve.tensor_tensor(x[:], ab[:, :, 0:16], dt[:].unsqueeze(1).broadcast_to([P, NT, 16]), ALU.add
                                  ).then_inc(s["x_done"], 1)
                dve.wait_ge(s["x_done"], 1)
                dve.wait_ge(s["lned"], 1)
                dve.wait_ge(s["aled"], 1)
                chain(dve.scalar_tensor_tensor(x[:], x[:], 0.0, e[:], ALU.max, ALU.add))
                chain(dve.tensor_tensor(x[:], x[:], rowmask[:].unsqueeze(2).broadcast_to([P, NT, 16]), ALU.mult))
                dve.scalar_tensor_tensor(t.g[:], x[:], -1.0, al[:].unsqueeze(1).broadcast_to([P, NT, 16]),
                                         ALU.mult, ALU.mult).then_inc(s["g_done"], 1)
                dve.wait_ge(s["g_done"], 1)
                dve.tensor_tensor(gseq[:], t.g[0:NS, NPT, :].unsqueeze(1).broadcast_to([NS, DECB, 16]),
                                  own[:].unsqueeze(2).broadcast_to([NS, DECB, 16]), ALU.mult).then_inc(s["g_done"], 1)
                dve.wait_ge(s["sums_done"], 2)
                for n, r in ((P, slice(0, NPT)), (NS, slice(NPT, NT))):
                    cut = lambda b: ps[b][0:n, r.start * 16:r.stop * 16].rearrange("p (t h) -> p t h", h=16)
                    chain(dve.tensor_copy(t.G[0:n, r, :], cut(1)))
                    chain(dve.tensor_tensor(t.kdec[0:n, r, :], cut(2), t.G[0:n, r, :], ALU.subtract))
                dve.sem_inc(s["dif_done"], 1)
                dve.wait_ge(s["out_done"], 1)
                dve.wait_ge(s["beta_done"], 1)
                chain(dve.tensor_tensor(t.beG[:], t.eG[:], t.beta[:], ALU.mult))


def delta(core, t, masks):
    nc, d, ps = core.nc, core.dram, core.ps
    G = HEADS
    UN = 21
    HALF = NTOK // 2
    PRE = 3 + SEQ + DECB * 7
    LV = [7, 7, 7, 7, 2]
    with Stage(core, "dn") as st:
        pre, y = st.sb("pre", [P, 2, PRE]), st.sb("y", [P, PRE])
        va, qr = st.sb("va", [P, 2, 4, NTOK]), st.sb("qr", [P, 2, 4, NTOK])
        z = st.sb("z", [P, NT, W])
        sq, ss, rs = st.sb("sq", [P, 4, P]), st.sb("ss", [P, 4]), st.sb("rs", [P, 4])
        qs4 = masks["qscale"]
        qkn, qkT = st.sb("qkn", [P, 4, P]), st.sb("qkT", [P, 2, 4, P])
        Rv, Rw, kd = (st.sb(n, [P, 2, 4, P]) for n in ("Rv", "Rw", "kd"))
        Gd, dm, dx = (st.sb(n, [P, 4, P]) for n in ("Gd", "dm", "dx"))
        att, TT = st.sb("att", [P, 2, 4, P]), st.sb("TT", [P, 2, 4, P])
        A, T, X = st.sb("A", [P, 2, 4, P]), st.sb("T", [P, 4, P]), st.sb("X", [P, 4, P])
        wT, u, S = st.sb("wT", [P, 4, P]), st.sb("u", [P, 4, P]), st.sb("S", [P, 4, P])
        ob, sqo, sso, rso = st.sb("ob", [P, 4, P]), sq, st.sb("sso", [P, 4]), st.sb("rso", [P, 4])
        sqo = st.sb("sqo", [P, 4, P])
        oTr = st.sb("oTr", [P, 2, 4, P])
        cv = oTr[:].rearrange("p v h f -> p v (h f)")
        SS = st.sb("SS", [P, 2, DECB, P])
        uq, us, ue = st.sb("uq", [P, 2 * NS]), st.sb("us", [NS, 2, 4, P]), st.sb("ue", [NS, DECB, P])
        cst = st.sb("cst", [P, 32, 27])
        ng = st.sb("ng", [P, P])
        names = ("ins", "zeroed", "pre_parts", "conv_done", "cst_done", "act_done", "z_taken", "zg_done", "dsteps", "psteps",
                 "a1", "a2", "a3", "a4", "a5", "sq_done", "ss_done", "rs_done", "qkn_done", "qkT_kept", "kd_done", "rv_done",
                 "gd_done", "dif_done", "dmx_done", "exp_done", "masked", "att_done", "A_done", "T_start", "x_ps0", "x_ps1", "xk0", "xk1",
                 "p_ps0", "p_ps1", "lv_done0", "lv_done1", "c1_ps", "wT_done", "u_ps", "u_done", "qs_ps", "qs_taken", "ds_ps", "av_ps", "o_done",
                 "S_done", "S_out", "sqo_done", "sso_done", "rso_done", "og_done", "oT_ps", "oT_kept", "oT_out0", "oT_out1",
                 "ss_in0", "ss_in1", "ss_out0", "ss_out1", "cs1_ps", "uq_done", "cs2_ps", "us_done", "ue_done", "ssc_done",
                 "cs3_ps", "sss_done", "cv_ps", "cv_kept", "cv_out0", "cv_out1")
        s = {n: st.sem(n) for n in names}

        def zi(x, l):
            return 30 * (x // NT) + 7 * (x % NT) + l

        def yi(x, l):
            return 25 * (x // NT) + 6 * (x % NT) + l - 1

        def a_steps(x):
            return [(n, x) for n in ("A1", "A4", "A2", "A3", "A5")]

        def b_steps(x):
            out = [("M", x)] + [("X", x, (0, r)) for r in range(2)]
            for l in range(1, LV[x % NT]):
                out += [(what, x, (l, r)) for what in ("X", "P") for r in range(2)]
            return out

        def c_steps(x):
            if x % NT < NPT:
                return [("C1", x), ("C2", x), ("C3", x), ("C4", x)]
            out = [("C1", x)]
            for h in range(4):
                out += [("S1", x, h), ("S2", x, h), ("S3", x, h)]
            return out + [("SO", x), ("C4", x)]

        def merge(*lists, at=None):
            keyed = []
            for n, a in enumerate(lists):
                if at and at[n] and len(a) == len(at[n]):
                    keyed += [(p, n, v) for p, v in zip(at[n], a)]
                else:
                    keyed += [((i + 0.5) / len(a), n, v) for i, v in enumerate(a)]
            return [v for _, _, v in sorted(keyed, key=lambda k: k[0])]

        def schedule():
            places = ((0.15, 0.3, 0.55, 0.7, 0.85), None, (0.02, 0.25, 0.48, 0.8))
            for g in range(G + 1):
                steps = []
                if g > 0:
                    for r in range(NT + 2):
                        xs = [5 * (g - 1) + r - i for i in range(3)]
                        now = [(f, x, p) for f, x, p, i in zip((a_steps, b_steps, c_steps), xs, places, range(3))
                               if 0 <= r - i < NT]
                        steps += merge(*[f(x) for f, x, _ in now], at=[p for _, _, p in now])
                mm = [("mm", UN * g + u, k) for u in range(UN) for k in range(KD)] if g < G else []
                tail = 2 * KD if steps else len(mm)
                yield from merge(steps, mm[:len(mm) - tail]) if steps else []
                yield from mm[len(mm) - tail:] if mm else []

        def unit(U):
            g, r = U // UN, U % UN
            if r < 16:
                return g, r // 8, (r % 8) // 2, r % 2
            return g, 2, r - 16, 0

        def fc(g, b, c):
            return 8 * g + 4 * b + c

        def channel(g, b, c):
            return 16 + 4 * g + c if b == 0 else (2 * g + c if c < 2 else 8 + 2 * g + c - 2)

        def taken(U):
            g, b, c, half = unit(U)
            if b == 2:
                return s["z_taken"], NT * g + c + 1
            return s["pre_parts"], 4 * fc(g, b, c) + 2 + 2 * half

        LATE = 3

        def follow(project, step, later=None, late=LATE):
            for item in schedule():
                if item[0] == "mm":
                    if item[2] == KD - 1:
                        project(item[1])
                    if later and item[2] == late and item[1] > 0:
                        later(item[1] - 1)
                else:
                    step(item[0], item[1], item[2] if len(item) > 2 else None)

        with nc.Block() as block:
            @block.sync
            def _(sp):
                sp.dma_start(ng[:], d["dn_norm_g"].broadcast_to([P, P])).then_inc(s["ins"], 16)
                oTd = d["oT"]

                def state_in(q):
                    if q >= 2:
                        sp.wait_ge(s[f"ss_out{q % 2}"], 16 * (q // 2))
                    sp.dma_start(SS[:, q % 2], d["state_dn"][0, :, q].rearrange("b p v -> p b v")).then_inc(s[f"ss_in{q % 2}"], 16)
                state_in(0)
                state_in(1)
                first = {UN * g + u: j for g in range(G) for j, u in enumerate((0, 8, 16))}

                def step(what, x, h):
                    g, i = x // NT, x % NT
                    if what == "C4":
                        sp.wait_ge(s["oT_kept"], x + 1)
                        sp.dma_start(oTd[:, 4 * g:4 * g + 4, tok(i)], oTr[:, x % 2, :, 0:rows(i)]).then_inc(s[f"oT_out{x % 2}"], 16)
                    if what == "C3" and i == NPT - 1:
                        sp.wait_ge(s["S_done"], 4 * NPT * (g + 1))
                        sp.dma_start(d["dn_p"][0, 0, 4 * g:4 * g + 4].rearrange("h p v -> p h v"), S[:]).then_inc(s["S_out"], 16)
                    if what == "S3":
                        q = 4 * g + h
                        sp.wait_ge(s["sss_done"], 2 * (q + 1))
                        sp.dma_start(d["dn_s"][0, :, q].rearrange("b p v -> p b v"), SS[:, q % 2]).then_inc(s[f"ss_out{q % 2}"], 16)
                        if q + 2 < 16:
                            state_in(q + 2)

                for item in schedule():
                    if item[0] == "mm":
                        if item[2] == 0 and item[1] in first and item[1] > 0:
                            core.mixer_weights(sp, 1)
                    else:
                        step(item[0], item[1], item[2] if len(item) > 2 else None)
                core.mixer_weights(sp, 1)
                for k in range(2):
                    sp.wait_ge(s[f"ss_out{k}"], 16 * 8)
                    sp.wait_ge(s[f"oT_out{k}"], 16 * 10)
                sp.wait_ge(s["S_out"], 16 * G)
                for j in range(8):
                    sp.wait_ge(s["cv_kept"], j + 1)
                    cols = slice(W * j, W * (j + 1))
                    sp.dma_start(d["conv_p"][0, 0, :, cols], cv[0:3, j % 2, :]).then_inc(s[f"cv_out{j % 2}"], 16)
                    sp.dma_start(d["conv_s"][0, :, :, cols].rearrange("b r c -> (b r) c"), cv[3:27, j % 2, :]
                                 ).then_inc(s[f"cv_out{j % 2}"], 16)
                for k in range(2):
                    sp.wait_ge(s[f"cv_out{k}"], 16 * 8)

            @block.tensor
            def _(pe):
                ident, ones = core.ident, core.ones

                def product(U, k):
                    g, b, c, half = unit(U)
                    w = core.base[1] + 3 * g + b
                    if k == 0:
                        pe.wait_ge(*core.arrival(w))
                        if U >= 2:
                            pe.wait_ge(*taken(U - 2))
                    if b == 2:
                        mm = pe.matmul(ps[U % 2][0:rows(c), :], core.hT[:, k, tok(c)], core.ring[:, w % RING, k, :],
                                       start=(k == 0), stop=(k == KD - 1))
                    else:
                        mm = pe.matmul(ps[U % 2][:, 0:HALF], core.ring[:, w % RING, k, c * P:(c + 1) * P],
                                       core.hT[:, k, half * HALF:(half + 1) * HALF], start=(k == 0), stop=(k == KD - 1))
                    if k == KD - 1:
                        mm.then_inc(core.proj_done[1], 1)

                def step(what, x, l):
                    g, i = x // NT, x % NT
                    n, v = rows(i), x % 2
                    if what == "A1":
                        pe.wait_ge(s["act_done"], 16 * (g + 1))
                        if x:
                            pe.wait_ge(s["A_done"], 4 * x)
                            pe.wait_ge(s["att_done"], x)
                        for c in range(4):
                            last = pe.transpose(ps[2][0:n, c * P:(c + 1) * P], qr[:, g % 2, c, tok(i)], ident[:, :])
                        last.then_inc(s["a1"], 1)
                    if what == "A2":
                        pe.wait_ge(s["qkn_done"], x + 1)
                        pe.wait_ge(s["dif_done"], x + 1)
                        for c in range(4):
                            last = pe.transpose(ps[3][:, c * n:(c + 1) * n], qkn[0:n, c, :], ident[0:n, 0:n])
                        last.then_inc(s["a2"], 1)
                    if what == "A3":
                        pe.wait_ge(s["qkn_done"], x + 1)
                        for c in range(4):
                            last = pe.transpose(ps[2][0:n, c * P:(c + 1) * P], va[:, g % 2, c, tok(i)], ident[:, :])
                        last.then_inc(s["a3"], 1)
                    if what == "A4":
                        pe.wait_ge(s["gd_done"], x + 1)
                        if x:
                            pe.wait_ge(s["qkT_kept"], x)
                        pe.matmul(ps[3][0:n, 0:4 * n], ones[0:n, 0:n], Gd[0:n, :, 0:n], start=True, stop=True
                                  ).then_inc(s["a4"], 1)
                    if what == "A5":
                        pe.wait_ge(s["rv_done"], x + 1)
                        pe.wait_ge(s["qkT_kept"], x + 1)
                        for a in range(2):
                            k = qkT[:, v, 2 + a, 0:n]
                            pe.matmul(ps[2][0:n, a * n:(a + 1) * n], k, k, start=True, stop=True)
                            last = pe.matmul(ps[2][0:n, (2 + a) * n:(3 + a) * n], k, qkT[:, v, a, 0:n], start=True, stop=True)
                        last.then_inc(s["a5"], 1)
                    if what == "X":
                        zz, r = zi(x, l[0]), l[1]
                        if l[0] == 0:
                            pe.wait_ge(s["A_done"], 4 * (x + 1))
                        if zz:
                            pe.wait_ge(s[f"lv_done{r}"], 2 * zz)
                        for k in range(2):
                            h, c = 2 * r + k, 2 * (l[0] % 2) + k
                            out, a = ps[5 + r][0:n, c * n:(c + 1) * n], A[0:n, v, h, 0:n]
                            if l[0] == 0:
                                last = pe.transpose(out, a, ident[0:n, 0:n])
                            else:
                                last = pe.matmul(out, a, TT[0:n, v, h, 0:n], start=True, stop=True)
                        last.then_inc(s[f"x_ps{r}"], 1)
                    if what == "P":
                        l, r = l
                        pe.wait_ge(s[f"xk{r}"], yi(x, l) + 1)
                        if l == 1:
                            pe.wait_ge(s["T_start"], x + 1)
                        pe.wait_ge(s[f"lv_done{r}"], 2 * zi(x, l))
                        for k in range(2):
                            h, c = 2 * r + k, 2 * (1 - l % 2) + k
                            last = pe.matmul(ps[5 + r][0:n, c * n:(c + 1) * n], T[0:n, h, 0:n], X[0:n, h, 0:n],
                                             start=True, stop=True)
                        if l < LV[i] - 1:
                            for k in range(2):
                                h, c = 2 * r + k, 2 * (l % 2) + k
                                last = pe.matmul(ps[5 + r][0:n, c * n:(c + 1) * n], X[0:n, h, 0:n], T[0:n, h, 0:n],
                                                 start=True, stop=True)
                        last.then_inc(s[f"p_ps{r}"], 1)
                    if what == "C1":
                        for r in range(2):
                            pe.wait_ge(s[f"lv_done{r}"], 2 * zi(x, LV[i]))
                        pe.wait_ge(s["kd_done"], 2 * (x + 1))
                        if i > 0:
                            pe.wait_ge(s["S_done"], 4 * (NPT * g + i))
                            for h in range(4):
                                last = pe.matmul(ps[4][:, h * n:(h + 1) * n], Rw[0:n, v, h, :], TT[0:n, v, h, 0:n],
                                                 start=True, stop=True)
                            last.then_inc(s["c1_ps"], 1)
                    if what == "C2":
                        pe.wait_ge(s["rv_done"], x + 1)
                        if x:
                            pe.wait_ge(s["oT_kept"], x)
                        if i > 0:
                            pe.wait_ge(s["wT_done"], 4 * g + i)
                        for h in range(4):
                            out = ps[7][:, h * P:(h + 1) * P]
                            last = pe.matmul(out, TT[:, v, h, :], Rv[:, v, h, :], start=True, stop=(i == 0))
                            if i > 0:
                                last = pe.matmul(out, wT[:, h, :], S[:, h, :], start=False, stop=True)
                        last.then_inc(s["u_ps"], 1)
                        if i > 0:
                            for h in range(4):
                                last = pe.matmul(ps[4][:, h * P:(h + 1) * P], qkT[:, v, h // 2, :], S[:, h, :],
                                                 start=True, stop=True)
                            last.then_inc(s["qs_ps"], 1)
                    if what == "C3":
                        pe.wait_ge(s["u_done"], NPT * g + i + 1)
                        if i > 0:
                            pe.wait_ge(s["qs_taken"], 3 * g + i)
                        elif g > 0:
                            pe.wait_ge(s["sss_done"], 8 * g)
                        for h in range(4):
                            last = pe.matmul(ps[4][:, h * P:(h + 1) * P], kd[:, v, h, :], u[:, h, :], start=True, stop=True)
                        last.then_inc(s["ds_ps"], 1)
                        for h in range(4):
                            last = pe.matmul(ps[7][:, h * P:(h + 1) * P], att[:, v, h, :], u[:, h, :], start=True, stop=True)
                        last.then_inc(s["av_ps"], 1)
                    if what == "S1":
                        q = 4 * g + l
                        pe.wait_ge(s[f"ss_in{q % 2}"], 16 * (q // 2 + 1))
                        pe.wait_ge(s["wT_done"], 4 * g + 4)
                        if l:
                            pe.wait_ge(s["sss_done"], 2 * q)
                        pe.matmul(ps[4][:, 0:NS], Rv[0:NS, v, l, :], TT[0:NS, v, l, 0:NS], start=True, stop=True)
                        for b in range(DECB):
                            c = slice(DECL * b, DECL * (b + 1))
                            pe.matmul(ps[4][:, c], SS[:, q % 2, b, :], wT[:, l, c], start=False, stop=True,
                                      skip_group_check=True)
                        for b in range(DECB):
                            c = slice(DECL * b, DECL * (b + 1))
                            last = pe.matmul(ps[4][:, NS + DECL * b:NS + DECL * (b + 1)], SS[:, q % 2, b, :],
                                             qkT[:, v, l // 2, c], start=True, stop=True)
                        last.then_inc(s["cs1_ps"], 1)
                    if what == "S2":
                        q = 4 * g + l
                        pe.wait_ge(s["uq_done"], q + 1)
                        if l == 0:
                            pe.wait_ge(s["oT_kept"], x)
                        for k in range(2):
                            last = pe.transpose(ps[7][0:NS, k * P:(k + 1) * P], uq[:, k * NS:(k + 1) * NS], ident[:, :])
                        last.then_inc(s["cs2_ps"], 1)
                    if what == "S3":
                        q = 4 * g + l
                        pe.wait_ge(s["ue_done"], q + 1)
                        for k in range(2):
                            last = pe.matmul(ps[4 + 3 * k][:, :], kd[0:NS, v, l, :], ue[:, 4 * k:4 * k + 4, :],
                                             start=True, stop=True)
                        last.then_inc(s["cs3_ps"], 1)
                    if what == "SO":
                        pe.wait_ge(s["sss_done"], 8 * (g + 1))
                        for h in range(4):
                            last = pe.matmul(ps[7][0:NS, h * P:(h + 1) * P], att[0:NS, v, h, 0:NS], us[:, 0, h, :],
                                             start=True, stop=True)
                        last.then_inc(s["av_ps"], 1)
                    if what == "C4":
                        pe.wait_ge(s["og_done"], x + 1)
                        for h in range(4):
                            last = pe.transpose(ps[7][:, h * n:(h + 1) * n], ob[0:n, h, :], ident[0:n, 0:n])
                        last.then_inc(s["oT_ps"], 1)

                for item in schedule():
                    if item[0] == "mm":
                        product(item[1], item[2])
                    else:
                        step(item[0], item[1], item[2] if len(item) > 2 else None)
                pe.wait_ge(s["cst_done"], 32)
                pe.wait_ge(s["oT_kept"], NT * G)
                for j in range(8):
                    if j >= 2:
                        pe.wait_ge(s["cv_kept"], j - 1)
                    for c in range(4):
                        last = pe.transpose(ps[2 + j % 2][0:27, c * P:(c + 1) * P], cst[:, 4 * j + c, :], ident[:, :])
                    last.then_inc(s["cv_ps"], 1)

            @block.scalar
            def _(act):
                act.wait_ge(s["zeroed"], 1)

                def project(U):
                    g, b, c, half = unit(U)
                    act.wait_ge(core.proj_done[1], U + 1)
                    if b == 2:
                        n = rows(c)
                        if g:
                            act.wait_ge(s["og_done"], NT * (g - 1) + c + 1)
                        act.activation(z[0:n, c, :], ps[U % 2][0:n, :], ACT.Silu).then_inc(s["z_taken"], 1)
                        return
                    F, r = fc(g, b, c), fc(g, b, c) % 2
                    seqs = pre[:, r, 3 + SEQ:PRE].rearrange("p (b w) -> p b w", w=7)
                    if half == 0:
                        if F >= 2:
                            act.wait_ge(s["conv_done"], F - 1)
                            act.wait_ge(s["cst_done"], F - 1)
                        act.activation(seqs[:, :, 0:3], t.conv[:, channel(g, b, c), 4:28].rearrange("p (b w) -> p b w", w=3),
                                       ACT.Copy).then_inc(s["pre_parts"], 1)
                        act.activation(pre[:, r, 3:3 + HALF], ps[U % 2][:, 0:HALF], ACT.Copy).then_inc(s["pre_parts"], 1)
                        return
                    act.activation(pre[:, r, 3 + HALF:3 + SEQ], ps[U % 2][:, 0:SEQ - HALF], ACT.Copy).then_inc(s["pre_parts"], 1)
                    act.activation(seqs[:, :, 3:7], ps[U % 2][:, SEQ - HALF:HALF].rearrange("p (b w) -> p b w", w=DECL),
                                   ACT.Copy).then_inc(s["pre_parts"], 1)

                def convolved(U):
                    g, b, c, half = unit(U)
                    if b == 2 or half == 0:
                        return
                    act.wait_ge(s["conv_done"], fc(g, b, c) + 1)
                    to = (va, qr)[b][:, g % 2, c, :]
                    if g >= 2:
                        act.wait_ge(s["a3"], NT * (g - 1))
                    act.activation(to[:, 0:SEQ], y[:, 0:SEQ], ACT.Silu).then_inc(s["act_done"], 1)
                    act.activation(to[:, SEQ:NTOK].rearrange("p (b w) -> p b w", w=DECL),
                                   y[:, 3 + SEQ:PRE].rearrange("p (b w) -> p b w", w=7)[:, :, 0:DECL], ACT.Silu
                                   ).then_inc(s["act_done"], 1)

                def step(what, x, l):
                    g, i = x // NT, x % NT
                    n, v = rows(i), x % 2
                    if what == "A1":
                        act.wait_ge(s["a1"], x + 1)
                        if x:
                            act.wait_ge(s["ss_done"], x)
                        act.activation(sq[0:n], ps[2][0:n, :].rearrange("p (h f) -> p h f", h=4), ACT.Square
                                       ).then_inc(s["sq_done"], 1)
                    if what == "A2":
                        act.wait_ge(s["a2"], x + 1)
                        if x >= 2:
                            act.wait_ge(s["av_ps"], x - 1)
                        act.activation(qkT[:, v, :, 0:n], ps[3][:, 0:4 * n].rearrange("p (h f) -> p h f", h=4), ACT.Copy
                                       ).then_inc(s["qkT_kept"], 1)
                    if what == "A4":
                        act.wait_ge(s["dmx_done"], x + 1)
                        act.activation(dm[0:n, :, 0:n], dm[0:n, :, 0:n], ACT.Exp).then_inc(s["exp_done"], 1)
                        act.activation(dx[0:n, :, 0:n], dx[0:n, :, 0:n], ACT.Exp, scale=-1.0).then_inc(s["exp_done"], 1)
                    if what == "C1" and i > 0:
                        act.wait_ge(s["c1_ps"], 4 * g + i)
                        act.wait_ge(s["av_ps"], x)
                        act.activation(wT[:, :, 0:n], ps[4][:, 0:4 * n].rearrange("p (h f) -> p h f", h=4), ACT.Copy,
                                       scale=-1.0).then_inc(s["wT_done"], 1)
                    if what == "C2":
                        act.wait_ge(s["u_ps"], NPT * g + i + 1)
                        if x:
                            act.wait_ge(s["av_ps"], x)
                        act.activation(u[:], ps[7][:, :].rearrange("p (h f) -> p h f", h=4), ACT.Copy).then_inc(s["u_done"], 1)
                    if what in ("C3", "SO"):
                        act.wait_ge(s["o_done"], x + 1)
                        if x:
                            act.wait_ge(s["sso_done"], x)
                        act.activation(sqo[0:n], ob[0:n], ACT.Square).then_inc(s["sqo_done"], 1)
                    if what == "S1":
                        q = 4 * g + l
                        act.wait_ge(s["cs1_ps"], q + 1)
                        if q:
                            act.wait_ge(s["cs2_ps"], q)
                        act.activation(uq[:], ps[4][:, 0:2 * NS], ACT.Copy).then_inc(s["uq_done"], 1)
                    if what == "S2":
                        q = 4 * g + l
                        act.wait_ge(s["cs2_ps"], q + 1)
                        if l == 0 and g > 0:
                            act.wait_ge(s["o_done"], NT * g)
                        act.activation(us[:, :, l, :], ps[7][0:NS, 0:2 * P].rearrange("p (k f) -> p k f", k=2), ACT.Copy
                                       ).then_inc(s["us_done"], 1)
                    if what == "C4":
                        act.wait_ge(s["oT_ps"], x + 1)
                        if x >= 2:
                            act.wait_ge(s[f"oT_out{v}"], 16 * (x // 2))
                        act.activation(oTr[:, v, :, 0:n], ps[7][:, 0:4 * n].rearrange("p (h f) -> p h f", h=4), ACT.Copy
                                       ).then_inc(s["oT_kept"], 1)

                follow(project, step, convolved, KD - 1)
                for j in range(8):
                    act.wait_ge(s["cv_ps"], j + 1)
                    if j < 2:
                        act.wait_ge(s[f"oT_out{j}"], 16 * NT * G // 2)
                    else:
                        act.wait_ge(s[f"cv_out{j % 2}"], 32 * (j // 2))
                    act.activation(cv[0:27, j % 2, :], ps[2 + j % 2][0:27, :], ACT.Copy).then_inc(s["cv_kept"], 1)

            @block.gpsimd
            def _(pool):
                chain = Chain(pool, s["psteps"])
                pool.wait_ge(s["ins"], 16)
                for r in range(2):
                    last = pool.memset(pre[:, r, 0:3], 0.0)
                last.then_inc(s["zeroed"], 1)

                def project(U):
                    g, b, c, half = unit(U)
                    if b == 2:
                        n = rows(c)
                        pool.wait_ge(s["z_taken"], NT * g + c + 1)
                        zz = z[0:n, c, :].rearrange("p (h f) -> p h f", h=4)
                        pool.tensor_tensor(zz, zz, ng[0:n, :].unsqueeze(1).broadcast_to([n, 4, P]), ALU.mult
                                           ).then_inc(s["zg_done"], 1)
                    elif half == 1:
                        F, ch = fc(g, b, c), channel(g, b, c)
                        pool.wait_ge(s["pre_parts"], 4 * F + 4)
                        pool.tensor_copy(cst[:, ch, 0:3], pre[:, F % 2, SEQ:SEQ + 3])
                        pool.tensor_copy(cst[:, ch, 3:27].rearrange("p (b w) -> p b w", w=3),
                                         pre[:, F % 2, 3 + SEQ:PRE].rearrange("p (b w) -> p b w", w=7)[:, :, 4:7]
                                         ).then_inc(s["cst_done"], 1)

                def step(what, x, l):
                    g, i = x // NT, x % NT
                    n, v = rows(i), x % 2
                    hs = slice(4 * g, 4 * g + 4)
                    if what == "A1":
                        if x:
                            pool.wait_ge(s["a4"], x)
                        tri = masks["incl"] if i < NPT else masks["incl_s"]
                        pool.tensor_tensor(Gd[0:n, :, 0:n], tri[0:n, 0:n].unsqueeze(1).broadcast_to([n, 4, n]),
                                           t.g[0:n, i, hs].unsqueeze(2).broadcast_to([n, 4, n]), ALU.mult).then_inc(s["gd_done"], 1)
                        pool.wait_ge(s["ss_done"], x + 1)
                        if x:
                            pool.wait_ge(s["qkn_done"], x)
                        chain(pool.tensor_scalar(rs[0:n], ss[0:n], RMS_EPS, 1.0, ALU.add, ALU.mult))
                        chain(pool.tensor_tensor(rs[0:n], rs[0:n], qs4[0:n, :], ALU.mult))
                        pool.tensor_tensor(rs[0:n], rs[0:n], core.eps[0:n, 3:4].broadcast_to([n, 4]), ALU.pow
                                           ).then_inc(s["rs_done"], 1)
                    if what == "A2":
                        pool.wait_ge(s["qkn_done"], x + 1)
                        if x >= 2:
                            pool.wait_ge(s["av_ps"], x - 1)
                        kk = qkn[0:n, 2:4, :].unsqueeze(2).broadcast_to([n, 2, 2, P])
                        for to, tab in ((Rw, t.beG), (kd, t.kdec)):
                            last = pool.tensor_tensor(to[0:n, v].rearrange("p (a r) f -> p a r f", r=2), kk,
                                                      tab[0:n, i, hs].rearrange("p (a r) -> p a r", r=2).unsqueeze(3)
                                                      .broadcast_to([n, 2, 2, P]), ALU.mult)
                            last.then_inc(s["kd_done"], 1)
                    if what == "A4":
                        pool.wait_ge(s["exp_done"], 2 * (x + 1))
                        m = ("incl", "lower") if i < NPT else ("incl_s", "lower_s")
                        for k, (to, name) in enumerate(((dm, m[0]), (dx, m[1]))):
                            pool.tensor_tensor(to[0:n, :, 0:n], to[0:n, :, 0:n],
                                               masks[name][0:n, 0:n].unsqueeze(1).broadcast_to([n, 4, n]), ALU.mult
                                               ).then_inc(s["masked"], 1)
                    if what == "M":
                        pool.wait_ge(s["A_done"], 4 * (x + 1))
                        if x:
                            for r in range(2):
                                pool.wait_ge(s[f"p_ps{r}"], yi(x, 1))
                                pool.wait_ge(s[f"lv_done{r}"], 2 * zi(x, 0))
                        To = T[0:n, :, 0:n]
                        chain(pool.tensor_tensor(To, A[0:n, v, :, 0:n],
                                                 masks["levels"][0:n, 7, 0:n].unsqueeze(1).broadcast_to([n, 4, n]), ALU.mult))
                        pool.tensor_tensor(To, core.ident[0:n, 0:n].unsqueeze(1).broadcast_to([n, 4, n]), To,
                                           ALU.subtract).then_inc(s["T_start"], 1)
                    if what in ("C3", "SO"):
                        pool.wait_ge(s["sso_done"], x + 1)
                        if x:
                            pool.wait_ge(s["og_done"], x)
                        chain(pool.tensor_scalar(rso[0:n], sso[0:n], float(P) * RMS_EPS, 1.0 / P, ALU.add, ALU.mult))
                        pool.tensor_tensor(rso[0:n], rso[0:n], core.eps[0:n, 3:4].broadcast_to([n, 4]), ALU.pow
                                           ).then_inc(s["rso_done"], 1)
                    if what == "S1":
                        q = 4 * g + l
                        pool.wait_ge(s["cs1_ps"], q + 1)
                        pool.tensor_tensor(SS[:, q % 2], SS[:, q % 2], t.egls[:, :, q:q + 1].broadcast_to([P, DECB, P]), ALU.mult
                                           ).then_inc(s["ssc_done"], 1)

                follow(project, step)

            @block.vector
            def _(dve):
                chain = Chain(dve, s["dsteps"])
                ident4 = lambda n: core.ident[0:n, 0:n].unsqueeze(1).broadcast_to([n, 4, n])
                b4 = lambda b, n, w: ps[b][0:n, 0:4 * w].rearrange("p (h f) -> p h f", h=4)

                b2 = lambda b, n, k: ps[b][0:n, 2 * k * n:2 * (k + 1) * n].rearrange("p (h f) -> p h f", h=2)

                def convolve(U):
                    g, b, c, half = unit(U)
                    if b == 2 or half == 0:
                        return
                    F, ch = fc(g, b, c), channel(g, b, c)
                    dve.wait_ge(s["pre_parts"], 4 * F + 4)
                    if F:
                        dve.wait_ge(s["act_done"], 2 * F)
                    n = PRE - 3
                    chain(dve.tensor_scalar(y[:, 0:n], pre[:, F % 2, 0:n], t.conv[:, ch, 0:1], None, ALU.mult))
                    for k in range(1, 4):
                        ins = dve.scalar_tensor_tensor(y[:, 0:n], pre[:, F % 2, k:k + n], t.conv[:, ch, k:k + 1], y[:, 0:n],
                                                       ALU.mult, ALU.add)
                        if k < 3:
                            chain(ins)
                    ins.then_inc(s["conv_done"], 1)

                def step(what, x, l):
                    g, i = x // NT, x % NT
                    n, v = rows(i), x % 2
                    hs = slice(4 * g, 4 * g + 4)
                    bc = lambda a, w: a.unsqueeze(2).broadcast_to([n, 4, w])
                    if what == "A1":
                        dve.wait_ge(s["sq_done"], x + 1)
                        if x:
                            dve.wait_ge(s["rs_done"], x)
                        dve.tensor_reduce(ss[0:n], sq[0:n], AX.X, ALU.add).then_inc(s["ss_done"], 1)
                        if x:
                            dve.wait_ge(s["a2"], x)
                            dve.wait_ge(s["kd_done"], 2 * x)
                        dve.wait_ge(s["rs_done"], x + 1)
                        dve.tensor_tensor(qkn[0:n], b4(2, n, P), bc(rs[0:n], P), ALU.mult).then_inc(s["qkn_done"], 1)
                    if what == "A3":
                        dve.wait_ge(s["a3"], x + 1)
                        if x >= 2:
                            dve.wait_ge(s["av_ps"], x - 1)
                        dve.tensor_tensor(Rv[0:n, v], b4(2, n, P), bc(t.beta[0:n, i, hs], P), ALU.mult).then_inc(s["rv_done"], 1)
                    if what == "A4":
                        dve.wait_ge(s["a4"], x + 1)
                        if x:
                            dve.wait_ge(s["A_done"], 4 * x)
                            dve.wait_ge(s["att_done"], x)
                        dve.tensor_tensor(dm[0:n, :, 0:n], b4(3, n, n), bc(t.G[0:n, i, hs], n), ALU.subtract
                                          ).then_inc(s["dif_done"], 1)
                        dve.wait_ge(s["dif_done"], x + 1)
                        chain(dve.tensor_scalar(dx[0:n, :, 0:n], dm[0:n, :, 0:n], 0.0, None, ALU.max))
                        dve.tensor_scalar(dm[0:n, :, 0:n], dm[0:n, :, 0:n], 0.0, None, ALU.min).then_inc(s["dmx_done"], 1)
                    if what == "A5":
                        dve.wait_ge(s["a5"], x + 1)
                        dve.wait_ge(s["masked"], 2 * (x + 1))
                        if x >= 2:
                            dve.wait_ge(s["av_ps"], x - 1)
                        r4 = lambda a: a.rearrange("p (a r) f -> p a r f", r=2)
                        two = lambda o: ps[2][0:n, o * n:(o + 2) * n].rearrange("p (a f) -> p a f", a=2).unsqueeze(2)\
                            .broadcast_to([n, 2, 2, n])
                        dve.tensor_tensor(r4(att[0:n, v, :, 0:n]), two(2), r4(dm[0:n, :, 0:n]), ALU.mult).then_inc(s["att_done"], 1)
                        if x >= 2:
                            dve.wait_ge(s["T_start"], x - 1)
                            for r in range(2):
                                dve.wait_ge(s[f"x_ps{r}"], zi(x - 1, 0))
                        for h in range(4):
                            last = dve.scalar_tensor_tensor(A[0:n, v, h, 0:n], ps[2][0:n, (h // 2) * n:(h // 2 + 1) * n],
                                                            t.beta[0:n, i, 4 * g + h:4 * g + h + 1], dx[0:n, h, 0:n],
                                                            ALU.mult, ALU.mult)
                            last.then_inc(s["A_done"], 1)
                    if what in ("X", "P"):
                        l, r = l
                        hh, more, k = slice(2 * r, 2 * r + 2), l < LV[i] - 1, l % 2
                        To, TTo = T[0:n, hh, 0:n], TT[0:n, v, hh, 0:n]
                    if what == "X":
                        dve.wait_ge(s[f"x_ps{r}"], zi(x, l) + 1)
                        if l == 0 and x >= 2:
                            dve.wait_ge(s["av_ps"], x - 1)
                        block_mask = masks["levels"][0:n, l, 0:n].unsqueeze(1).broadcast_to([n, 2, n])
                        if l > 0:
                            dve.tensor_tensor(X[0:n, hh, 0:n], b2(5 + r, n, k), block_mask, ALU.mult).then_inc(s[f"xk{r}"], 1)
                        else:
                            chain(dve.tensor_tensor(TTo, b2(5 + r, n, k), block_mask, ALU.mult))
                            dve.tensor_tensor(TTo, core.ident[0:n, 0:n].unsqueeze(1).broadcast_to([n, 2, n]), TTo,
                                              ALU.subtract).then_inc(s[f"lv_done{r}"], 2)
                    if what == "P":
                        if l == 1:
                            dve.wait_ge(s["T_start"], x + 1)
                        dve.wait_ge(s[f"lv_done{r}"], 2 * zi(x, l))
                        dve.wait_ge(s[f"p_ps{r}"], yi(x, l) + 1)
                        dve.tensor_tensor(TTo, TTo, b2(5 + r, n, 1 - k), ALU.subtract
                                          ).then_inc(s[f"lv_done{r}"], 1 if more else 2)
                        if more:
                            dve.tensor_tensor(To, To, b2(5 + r, n, k), ALU.subtract).then_inc(s[f"lv_done{r}"], 1)
                    if what == "C2" and i > 0:
                        dve.wait_ge(s["qs_ps"], 3 * g + i)
                        if x:
                            dve.wait_ge(s["oT_ps"], x)
                        dve.tensor_tensor(ob[:], b4(4, P, P), bc(t.eG[:, i, hs], P), ALU.mult).then_inc(s["qs_taken"], 1)
                    if what == "C3":
                        dve.wait_ge(s["av_ps"], x + 1)
                        if i > 0:
                            dve.wait_ge(s["qs_taken"], 3 * g + i)
                            dve.tensor_tensor(ob[:], ob[:], b4(7, P, P), ALU.add).then_inc(s["o_done"], 1)
                        else:
                            if x:
                                dve.wait_ge(s["oT_ps"], x)
                            dve.tensor_copy(ob[:], b4(7, P, P)).then_inc(s["o_done"], 1)
                        dve.wait_ge(s["ds_ps"], NPT * g + i + 1)
                        if i == 0 and g > 0:
                            dve.wait_ge(s["S_out"], 16 * g)
                        if i > 0:
                            dve.wait_ge(s["S_done"], 4 * (NPT * g + i))
                        for h in range(4):
                            src = ps[4][:, h * P:(h + 1) * P]
                            if i == 0:
                                last = dve.tensor_copy(S[:, h, :], src)
                            else:
                                last = dve.scalar_tensor_tensor(S[:, h, :], S[:, h, :], t.egl[:, i, 4 * g + h:4 * g + h + 1], src,
                                                                ALU.mult, ALU.add)
                            last.then_inc(s["S_done"], 1)
                        normalise(x, i, n)
                    if what == "S2":
                        q = 4 * g + l
                        dve.wait_ge(s["us_done"], q + 1)
                        if q:
                            dve.wait_ge(s["cs3_ps"], q)
                        dve.tensor_tensor(ue[:], us[:, 0, l, :].unsqueeze(1).broadcast_to([NS, DECB, P]),
                                          masks["own"][:].unsqueeze(2).broadcast_to([NS, DECB, P]), ALU.mult).then_inc(s["ue_done"], 1)
                    if what == "S3":
                        q = 4 * g + l
                        dve.wait_ge(s["cs3_ps"], q + 1)
                        dve.wait_ge(s["ssc_done"], q + 1)
                        for k in range(2):
                            part = SS[:, q % 2, 4 * k:4 * k + 4, :]
                            dve.tensor_tensor(part, part, ps[4 + 3 * k][:, :].rearrange("p (b f) -> p b f", b=4), ALU.add
                                              ).then_inc(s["sss_done"], 1)
                    if what == "SO":
                        dve.wait_ge(s["oT_ps"], x)
                        chain(dve.tensor_tensor(ob[0:n], us[:, 1], bc(t.eG[0:n, i, hs], P), ALU.mult))
                        dve.wait_ge(s["av_ps"], x + 1)
                        dve.tensor_tensor(ob[0:n], ob[0:n], b4(7, n, P), ALU.add).then_inc(s["o_done"], 1)
                        normalise(x, i, n)

                def normalise(x, i, n):
                    dve.wait_ge(s["sqo_done"], x + 1)
                    if x:
                        dve.wait_ge(s["rso_done"], x)
                    dve.tensor_reduce(sso[0:n], sqo[0:n], AX.X, ALU.add).then_inc(s["sso_done"], 1)
                    dve.wait_ge(s["rso_done"], x + 1)
                    dve.wait_ge(s["zg_done"], x + 1)
                    chain(dve.tensor_tensor(ob[0:n], ob[0:n], rso[0:n].unsqueeze(2).broadcast_to([n, 4, P]), ALU.mult))
                    dve.tensor_tensor(ob[0:n], ob[0:n], z[0:n, i, :].rearrange("p (h f) -> p h f", h=4), ALU.mult
                                      ).then_inc(s["og_done"], 1)

                follow(lambda U: None, step, convolve)


def routing(core, l, hk, logits, plan):
    nc, d, ps = core.nc, core.dram, core.ps
    with Stage(core, f"route{l}") as st:
        f = lambda name, *shape: st.sb(name, [P, *shape])
        strict, bias, cw4, cw16, thr, before, tiles, rowmask = (
            f("strict", P), f("bias", NE), f("cw4", 4), f("cw16", NE), f("thr", NT), f("before", NE, NE),
            f("tiles", MAXT), f("rowmask", NT))
        mx, e, probs, sel = f("mx", NT), f("e", NT, NE), f("probs", NT, NE), f("sel", NT, NE)
        pairs, gs, geq = f("pairs", NT * 4, 6), f("gs", NT, 4), f("geq", NT, 4)
        one = [f("one0", NT, NE), f("one1", NT, NE)]
        t16, both, dest, w = f("t16", NT, NE), f("both", NT, NE), f("dest", NT, NE), f("w", 2, NT)
        cmp5, nt, start, t256 = f("cmp5", NE, NT), f("nt", NE), f("start", NE), f("t256", NE, NE)
        end, exp_t, exp_f = f("end", NE), f("exp_t", MAXT, NE), f("exp_f", MAXT + 1)
        consts, steps, shifted, exped, both_done, rank_done, placed = (
            st.sem(n) for n in ("consts", "steps", "shifted", "exped", "both_done", "rank_done", "placed"))
        sent = st.pool_sem("rows_sent")
        with nc.Block() as block:
            @block.sync
            def _(sp):
                for to, name in ((strict, "c_strict"), (cw4, "c_cw4"), (cw16, "c_cw16"), (thr, "c_thr"),
                                 (before, "c_before"), (tiles, "c_tiles"), (rowmask, "c_rowmask")):
                    sp.dma_start(to[:], d[name]).then_inc(consts, 16)
                sp.dma_start(bias[:], d["router_b"].rearrange("(o e) -> o e", o=1).broadcast_to([P, NE])
                             ).then_inc(consts, 16)

            @block.scalar
            def _(act):
                act.wait_ge(shifted, 1)
                act.activation(e[:], e[:], ACT.Exp).then_inc(exped, 1)

            @block.tensor
            def _(pe):
                pe.wait_ge(both_done, 1)
                for t in range(NT + 1):
                    out = ps[0][:, t * NE:(t + 1) * NE]
                    for u in range(min(t + 1, NT)):
                        last = pe.matmul(out, strict[:, :] if u == t else core.ones[:, :], both[:, u, :],
                                         start=(u == 0), stop=(u == min(t, NT - 1)))
                last.then_inc(rank_done, 1)

            @block.vector
            def _(dve):
                chain = Chain(dve, steps)
                dve.wait_ge(consts, 16 * 8)
                bc = lambda a, n: a.unsqueeze(2).broadcast_to([P, a.shape[1], n])
                row = lambda a, n: a.unsqueeze(1).broadcast_to([P, n, a.shape[1]])
                chain(dve.tensor_reduce(mx[:], logits[:], AX.X, ALU.max))
                dve.tensor_tensor(e[:], logits[:], bc(mx[:], NE), ALU.subtract).then_inc(shifted, 1)
                dve.wait_ge(exped, 1)
                chain(dve.tensor_reduce(mx[:], e[:], AX.X, ALU.add))
                chain(dve.reciprocal(mx[:], mx[:]))
                chain(dve.tensor_tensor(probs[:], e[:], bc(mx[:], NE), ALU.mult))
                chain(dve.tensor_tensor(sel[:], probs[:], row(bias[:], NT), ALU.add))
                g4 = sel[:].rearrange("p t (g e) -> p (t g) e", g=4)
                chain(dve.tensor_tensor(pairs[:, :, 0:3], g4[:, :, 0:3], g4[:, :, 1:4], ALU.add))
                chain(dve.tensor_tensor(pairs[:, :, 3:5], g4[:, :, 0:2], g4[:, :, 2:4], ALU.add))
                chain(dve.tensor_tensor(pairs[:, :, 5:6], g4[:, :, 0:1], g4[:, :, 3:4], ALU.add))
                chain(dve.tensor_reduce(gs[:].rearrange("p t g -> p (t g)"), pairs[:], AX.X, ALU.max))

                def first_best(values, weights, n, out):
                    chain(dve.tensor_reduce(mx[:], values, AX.X, ALU.max))
                    chain(dve.tensor_tensor(out, values, bc(mx[:], n), ALU.is_ge))
                    chain(dve.tensor_tensor(out, out, row(weights, NT), ALU.mult))
                    chain(dve.tensor_reduce(mx[:], out, AX.X, ALU.max))
                    chain(dve.tensor_tensor(out, out, bc(mx[:], n), ALU.is_equal))

                first_best(gs[:], cw4[:], 4, geq[:])
                chain(dve.tensor_scalar(geq[:], geq[:], 1e30, -1e30, ALU.mult, ALU.add))
                for t in range(NT):
                    last = dve.tensor_tensor(sel[:, t, :].rearrange("p (g e) -> p g e", g=4),
                                             sel[:, t, :].rearrange("p (g e) -> p g e", g=4),
                                             geq[:, t, :].unsqueeze(2).broadcast_to([P, 4, 4]), ALU.add)
                    chain.mark(last)
                dve.wait_ge(steps, chain.n)
                first_best(sel[:], cw16[:], NE, one[0][:])
                chain(dve.scalar_tensor_tensor(sel[:], one[0][:], -2e30, sel[:], ALU.mult, ALU.add))
                first_best(sel[:], cw16[:], NE, one[1][:])
                chain(dve.tensor_tensor(both[:], one[0][:], one[1][:], ALU.add))
                dve.tensor_tensor(both[:], both[:], bc(rowmask[:], NE), ALU.mult).then_inc(both_done, 1)
                for j in range(2):
                    chain(dve.tensor_tensor(t16[:], probs[:], one[j][:], ALU.mult))
                    chain(dve.tensor_reduce(w[:, j, :], t16[:], AX.X, ALU.add))
                chain(dve.tensor_tensor(mx[:], w[:, 0, :], w[:, 1, :], ALU.add))
                chain(dve.reciprocal(mx[:], mx[:]))
                chain(dve.tensor_tensor(plan.weight[:], w[:], mx[:].unsqueeze(1).broadcast_to([P, 2, NT]), ALU.mult))
                dve.wait_ge(rank_done, 1)
                chain(dve.tensor_copy(dest[:], ps[0][:, 0:NT * NE].rearrange("p (t e) -> p t e", t=NT)))
                chain(dve.tensor_copy(nt[:], ps[0][:, NT * NE:(NT + 1) * NE]))
                chain(dve.tensor_tensor(cmp5[:], bc(nt[:], NT), row(thr[:], NE), ALU.is_gt))
                chain(dve.tensor_reduce(nt[:], cmp5[:], AX.X, ALU.add))
                chain(dve.tensor_tensor(t256[:], row(nt[:], NE), before[:], ALU.mult))
                chain(dve.tensor_reduce(start[:], t256[:], AX.X, ALU.add))
                chain(dve.tensor_tensor(end[:], start[:], nt[:], ALU.add))
                chain(dve.tensor_scalar(start[:], start[:], float(P), None, ALU.mult))
                chain(dve.tensor_tensor(dest[:], dest[:], row(start[:], NT), ALU.add))
                for j in range(2):
                    chain(dve.tensor_tensor(t16[:], dest[:], one[j][:], ALU.mult))
                    chain(dve.tensor_reduce(w[:, j, :], t16[:], AX.X, ALU.add))
                dve.tensor_copy(plan.place[:], w[:]).then_inc(placed, 1)
                chain(dve.tensor_tensor(exp_t[:], row(end[:], MAXT), bc(tiles[:], NE), ALU.is_le))
                chain(dve.tensor_reduce(exp_f[:, 0:MAXT], exp_t[:], AX.X, ALU.add))
                chain(dve.tensor_scalar(exp_f[:, 0:MAXT], exp_f[:, 0:MAXT], float(NE - 1), None, ALU.min))
                chain(dve.tensor_scalar(exp_t[:, 0:MAXT // 2, 0:1], tiles[:].rearrange("p (a b) -> p a b", b=2)[:, :, 0:1],
                                        end[:, NE - 1:NE], None, ALU.is_lt))
                chain(dve.tensor_reduce(exp_f[:, MAXT:MAXT + 1], exp_t[:, 1:MAXT // 2, 0:1].rearrange("p a b -> p (a b)"),
                                        AX.X, ALU.add))
                chain(dve.tensor_copy(plan.experts[:], exp_f[0:1, :]))

            @block.gpsimd
            def _(pool):
                pool.wait_ge(placed, 1)
                for t in range(NT):
                    for j in range(2):
                        pool.indirect_dma_start(
                            out=d["rows"], out_offset=bass.IndirectOffsetOnAxis(ap=plan.place[0:rows(t), j, t:t + 1], axis=0),
                            in_=hk[0:rows(t), t, :], in_offset=None).then_inc(sent, 16)
                pool.wait_ge(sent, 16 * 2 * NT)


def experts(core, l, plan):
    nc, d, ps = core.nc, core.dram, core.ps
    flat = core.ring[:].rearrange("p r k n -> p (r k n)")
    wgu = [flat[:, i * KD * W:(i + 1) * KD * W].rearrange("p (k n) -> p k n", k=KD) for i in range(2)]
    wdn = [flat[:, 2 * KD * W + i * 2 * D:2 * KD * W + (i + 1) * 2 * D].rearrange("p (k n) -> p k n", k=2)
           for i in range(2)]
    with Stage(core, f"exp{l}") as st:
        x, xT = st.sb("x", [P, 2, D]), st.sb("xT", [P, 2, KD, P])
        sg, a, aT = st.sb("sg", [P, 2, DE]), st.sb("a", [P, 2, DE]), st.sb("aT", [P, 2, 2, P])
        y = st.sb("y", [P, 2, D])
        names = ("x_in0", "x_in1", "gu_in0", "gu_in1", "dn_in0", "dn_in1", "turned", "xT_kept", "gu_done", "silu_done",
                 "a_done", "aT_turned", "aT_kept", "y_done", "y_kept_act", "y_kept_dve", "y_free")
        s = {n: st.sem(n) for n in names}
        s["y_out0"], s["y_out1"] = st.pool_sem("expert_rows_out0"), st.pool_sem("expert_rows_out1")
        gu = d["moe_w_gu"][l].rearrange("e (k p) f -> p e k f", p=P)
        dn = d["moe_w_down"][l].rearrange("e (k p) n -> p e k n", p=P)
        xr = d["rows"].rearrange("(s p) n -> p s n", p=P)
        yr = d["y_rows"].rearrange("(s p) n -> p s n", p=P)

        def tiles(eng, step, first=0):
            last = eng.value_load(plan.experts[0:1, MAXT:MAXT + 1], min_val=1, max_val=MAXT // 2 - 1)
            for v in range(2):
                step(v, v, 0, True)
            with eng.Fori(1, last + 1) as p:
                for v in range(2):
                    step(p * 2 + v, v, p, False)
            return last

        with nc.Block() as block:
            @block.sync
            def _(sp):
                def step(i, v, p, early):
                    e = sp.value_load(plan.experts[0:1, bass.ds(i, 1)] if not early else plan.experts[0:1, i:i + 1],
                                      min_val=0, max_val=NE - 1)
                    if not early:
                        sp.wait_ge(s["turned"], i - 1)
                    sp.dma_start(x[:, v, :], xr[:, bass.ds(i, 1), :]).then_inc(s[f"x_in{v}"], 16)
                    if not early:
                        sp.wait_ge(s["gu_done"], i - 1)
                    sp.dma_start(wgu[v], gu[:, bass.ds(e, 1)].rearrange("p e k f -> p (e k) f")).then_inc(s[f"gu_in{v}"], 16)
                    if not early:
                        sp.wait_ge(s["y_done"], i)
                    sp.dma_start(wdn[v], dn[:, bass.ds(e, 1)].rearrange("p e k f -> p (e k) f")).then_inc(s[f"dn_in{v}"], 16)
                tiles(sp, step)

            def turn(pe, i, v, p, early):
                pe.wait_ge(s[f"x_in{v}"], p * 16 + 16)
                if not (early and v == 0):
                    pe.wait_ge(s["xT_kept"], i * 2)
                for k in range(KD):
                    last = pe.transpose(ps[4 + k // 4][:, (k % 4) * P:(k % 4 + 1) * P], x[:, v, k * P:(k + 1) * P],
                                        core.ident[:, :])
                last.then_inc(s["turned"], 1)

            def up(pe, i, v, p, early):
                pe.wait_ge(s["xT_kept"], i * 2 + 2)
                pe.wait_ge(s[f"gu_in{v}"], p * 16 + 16)
                if not early:
                    pe.wait_ge(s["a_done"], i - 1)
                for k in range(KD):
                    last = pe.matmul(ps[v][:, :], xT[:, v, k, :], wgu[v][:, k, :], start=(k == 0), stop=(k == KD - 1))
                last.then_inc(s["gu_done"], 1)

            def turn_a(pe, i, v, early):
                pe.wait_ge(s["a_done"], i + 1)
                if not (early and v == 0):
                    pe.wait_ge(s["aT_kept"], i)
                for k in range(2):
                    last = pe.transpose(ps[6][:, k * P:(k + 1) * P], a[:, v, k * P:(k + 1) * P], core.ident[:, :])
                last.then_inc(s["aT_turned"], 1)

            def down(pe, i, v, p1, early):
                pe.wait_ge(s["aT_kept"], i + 1)
                pe.wait_ge(s[f"dn_in{v}"], p1 * 16)
                pe.wait_ge(s["y_kept_act"], i + 1)
                pe.wait_ge(s["y_kept_dve"], i + 1)
                for c in range(2):
                    for k in range(2):
                        last = pe.matmul(ps[2 + c][:, :], aT[:, v, k, :], wdn[v][:, k, c * W:(c + 1) * W],
                                         start=(k == 0), stop=(k == 1))
                last.then_inc(s["y_done"], 1)

            @block.tensor
            def _(pe):
                def step(i, v, p, early):
                    turn(pe, i, v, p, early)
                    if not early:
                        down(pe, i - 2, v, p, False)
                    if not early or v == 1:
                        turn_a(pe, i - 1, 1 - v, early)
                    up(pe, i, v, p, early)
                pe.sem_inc(s["y_done"], 1)
                last = tiles(pe, step)
                down(pe, last * 2, 0, last + 1, False)
                turn_a(pe, last * 2 + 1, 1, False)
                down(pe, last * 2 + 1, 1, last + 1, False)
                pe.nop()

            def y_keep(eng, i, v, half):
                eng.wait_ge(s["y_done"], i + 2)
                eng.wait_ge(s["y_free"], i + 1)
                if half == 0:
                    eng.activation(y[:, v, 0:W], ps[2][:, :], ACT.Copy).then_inc(s["y_kept_act"], 1)
                else:
                    eng.tensor_copy(y[:, v, W:D], ps[3][:, :]).then_inc(s["y_kept_dve"], 1)

            @block.scalar
            def _(act):
                def keep_a(i, v, early):
                    act.wait_ge(s["aT_turned"], i + 1)
                    if not early:
                        act.wait_ge(s["y_done"], i)
                    act.activation(aT[:, v], ps[6][:, 0:2 * P].rearrange("p (k n) -> p k n", k=2), ACT.Copy
                                   ).then_inc(s["aT_kept"], 1)

                def step(i, v, p, early):
                    act.wait_ge(s["turned"], i + 1)
                    if not early:
                        act.wait_ge(s["gu_done"], i - 1)
                    for h in range(2):
                        act.activation(xT[:, v, 4 * h:4 * h + 4, :], ps[4 + h][:, :].rearrange("p (k n) -> p k n", k=4),
                                       ACT.Copy).then_inc(s["xT_kept"], 1)
                    if not early:
                        y_keep(act, i - 2, v, 0)
                    if not early or v == 1:
                        keep_a(i - 1, 1 - v, early)
                    act.wait_ge(s["gu_done"], i + 1)
                    if not early:
                        act.wait_ge(s["a_done"], i - 1)
                    act.activation(sg[:, v, :], ps[v][:, 0:DE], ACT.Silu).then_inc(s["silu_done"], 1)

                act.sem_inc(s["y_kept_act"], 1)
                last = tiles(act, step)
                y_keep(act, last * 2, 0, 0)
                keep_a(last * 2 + 1, 1, False)
                y_keep(act, last * 2 + 1, 1, 0)
                act.nop()

            @block.vector
            def _(dve):
                def step(i, v, p, early):
                    if not early:
                        y_keep(dve, i - 2, v, 1)
                    dve.wait_ge(s["silu_done"], i + 1)
                    if not early:
                        dve.wait_ge(s["aT_turned"], i - 1)
                    dve.tensor_tensor(a[:, v, :], ps[v][:, DE:2 * DE], sg[:, v, :], ALU.mult).then_inc(s["a_done"], 1)
                dve.sem_inc(s["y_kept_dve"], 1)
                last = tiles(dve, step)
                y_keep(dve, last * 2, 0, 1)
                y_keep(dve, last * 2 + 1, 1, 1)
                dve.nop()

            @block.gpsimd
            def _(pool):
                pool.sem_inc(s["y_free"], 2)
                last = pool.value_load(plan.experts[0:1, MAXT:MAXT + 1], min_val=1, max_val=MAXT // 2 - 1)
                with pool.Fori(0, last + 1) as p:
                    for v in range(2):
                        pool.wait_ge(s["y_kept_act"], p * 2 + (v + 2))
                        pool.wait_ge(s["y_kept_dve"], p * 2 + (v + 2))
                        pool.dma_start(yr[:, bass.ds(p * 2 + v, 1), :], y[:, v, :]).then_inc(s[f"y_out{v}"], 16)
                        pool.wait_ge(s[f"y_out{v}"], p * 16 + 16)
                        pool.sem_inc(s["y_free"], 1)


def combine(core, l, plan, x_from, x_to, more):
    nc, d, ps = core.nc, core.dram, core.ps
    SLOTS = 3 if more else NT
    with Stage(core, f"comb{l}") as st:
        ya, yb = st.sb("ya", [P, SLOTS, D]), st.sb("yb", [P, SLOTS, D])
        h = st.sb("h", [P, 2, D]) if more else ya
        r = Residual(core, st, l, 1, more)
        s = {n: st.sem(n) for n in ("steps", "y_used", "weighed", "turned", "kept")}
        for t in range(NT):
            s[f"got{t}"] = st.pool_sem(f"outputs_got{t}")
        with nc.Block() as block:
            @block.sync
            def _(sp):
                r.gates(sp)
                r.load(sp, x_from)
                r.vectors(sp)
                if more:
                    sp.wait_ge(s[f"got{NT - 1}"], 32)
                    core.mixer_weights(sp, l + 1, RING)
                for t in range(NT):
                    r.store(sp, t, x_to)
                r.stored(sp)

            @block.gpsimd
            def _(pool):
                r.pchain = Chain(pool, r.psteps)

                def gather(t):
                    n, v = rows(t), t % SLOTS
                    if t >= SLOTS:
                        pool.wait_ge(s["y_used"], t - SLOTS + 1)
                    for j, to in ((0, ya), (1, yb)):
                        pool.indirect_dma_start(out=to[0:n, v, :], out_offset=None, in_=d["y_rows"],
                                                in_offset=bass.IndirectOffsetOnAxis(ap=plan.place[0:n, j, t:t + 1], axis=0)
                                                ).then_inc(s[f"got{t}"], 16)
                for t in range(SLOTS):
                    gather(t)
                r.deviation(pool, 0)
                for t in range(NT):
                    if t + 1 < NT:
                        r.deviation(pool, t + 1)
                    if t + SLOTS < NT:
                        gather(t + SLOTS)
                    r.outputs(pool, t)

            @block.vector
            def _(dve):
                chain = Chain(dve, s["steps"])
                def join(t):
                    n, v = rows(t), t % SLOTS
                    A, B = ya[0:n, v, :], yb[0:n, v, :]
                    dve.wait_ge(s["weighed"], t + 1)
                    chain(dve.scalar_tensor_tensor(A, B, plan.weight[0:n, 1, t:t + 1], A, ALU.mult, ALU.add))
                    r.join(dve, chain, t, [(slice(0, D), A, B)], None)
                    dve.sem_inc(s["y_used"], 1)

                join(0)
                if more:
                    r.fold_vectors(dve, chain, h[:, 0, :])
                for t in range(NT):
                    if t + 1 < NT:
                        join(t + 1)
                    if more and t >= 2:
                        dve.wait_ge(s["turned"], t - 1)
                    r.finish(dve, chain, t, h[0:rows(t), t % 2, :])

            if more:
                @block.tensor
                def _(pe):
                    for t in range(NT):
                        pe.wait_ge(r.h_done, t + 1)
                        if t >= 2:
                            pe.wait_ge(s["kept"], 2 * (t - 1))
                        turn_tile(pe, core, h[:, t % 2, :], t, (2 * (t % 2), 2 * (t % 2) + 1)).then_inc(s["turned"], 1)

            @block.scalar
            def _(act):
                def weigh(t):
                    n, v = rows(t), t % SLOTS
                    act.wait_ge(s[f"got{t}"], 32)
                    act.activation(ya[0:n, v, :], ya[0:n, v, :], ACT.Copy, scale=plan.weight[0:n, 0, t:t + 1]
                                   ).then_inc(s["weighed"], 1)
                weigh(0)
                weigh(1)
                for t in range(NT):
                    if t + 2 < NT:
                        weigh(t + 2)
                    if more:
                        act.wait_ge(s["turned"], t + 1)
                        keep_turned(act, core, t, (2 * (t % 2), 2 * (t % 2) + 1), s["kept"])


class Plan:

    def __init__(self, core, ctx, l):
        self.place = core.sb(ctx, f"place{l}", [P, 2, NT], U32)
        self.weight = core.sb(ctx, f"weight{l}", [P, 2, NT])
        self.experts = core.sb(ctx, f"experts{l}", [1, MAXT + 1], I32)


class Residual:

    def __init__(self, core, st, l, half, more):
        self.core, self.l, self.half, self.more = core, l, half, more
        self.x = st.sb("x", [P, NT, D])
        self.gate = st.sb("gate", [P, 2, D])
        self.g, self.b = st.sb("g", [P, D]), st.sb("b", [P, D])
        self.scale = st.sb("scale", [P, 2, D]) if more else None
        self.shift = st.sb("shift", [P, 2, D]) if more else None
        self.stats, self.mom = st.sb("stats", [P, 2, 2, 6]), st.sb("mom", [P, 2, 2])
        self.var, self.rstd = st.sb("var", [P, 2, 1]), st.sb("rstd", [P, 2, 1])
        self.vec_in, self.gate_in = st.sem("vec_in"), st.sem("gate_in")
        self.x_in = [st.sem(f"x_in{t}") for t in range(NT)]
        self.x_out = st.sem("x_out")
        self.moments, self.rstd_done, self.xn_used, self.x_done, self.h_done, self.psteps = (
            st.sem(n) for n in ("moments", "rstd_done", "xn_used", "x_done", "h_done", "psteps"))

    def gates(self, sp):
        vectors_in(sp, self.core.dram, self.l, 3 * self.half + 2, self.gate, self.gate_in)

    def vectors(self, sp):
        d, l = self.core.dram, self.l
        for to, name in ((self.g, "ln_g"), (self.b, "ln_b")):
            sp.dma_start(to[:, :], d[name][l, self.half:self.half + 1, :].broadcast_to([P, D])).then_inc(self.vec_in, 16)
        self.vec_total = 32
        if self.more:
            nl, part = (l, 3) if self.half == 0 else (l + 1, 0)
            vectors_in(sp, d, nl, part, self.shift, self.vec_in)
            vectors_in(sp, d, nl, part + 1, self.scale, self.vec_in)
            self.vec_total += 64

    def load(self, sp, source):
        for t in range(NT):
            sp.dma_start(self.x[0:rows(t), t, :], source(t)).then_inc(self.x_in[t], 16)

    def store(self, sp, t, dest):
        sp.wait_ge(self.x_done, t + 1)
        sp.dma_start(dest(t), self.x[0:rows(t), t, :]).then_inc(self.x_out, 16)

    def stored(self, sp):
        sp.wait_ge(self.x_out, 16 * NT)

    def deviation(self, pool, t):
        n, v = rows(t), t % 2
        pool.wait_ge(self.moments, t + 1)
        chain = self.pchain
        chain(pool.tensor_scalar(self.var[0:n, v, :], self.mom[0:n, v, 1:2], LN_EPS, 1.0, ALU.add, ALU.mult))
        pool.tensor_tensor(self.rstd[0:n, v, :], self.var[0:n, v, :], self.core.eps[0:n, 3:4], ALU.pow
                           ).then_inc(self.rstd_done, 1)

    def outputs(self, pool, t):
        n, v = rows(t), t % 2
        x, chain = self.x[0:n, t, :], self.pchain
        if t == 0:
            pool.wait_ge(self.vec_in, self.vec_total)
        pool.wait_ge(self.xn_used, t + 1)
        if self.more:
            chain(pool.tensor_tensor(x, x, self.g[0:n, :], ALU.mult))
        pool.tensor_tensor(x, x, self.b[0:n, :], ALU.add).then_inc(self.x_done, 1)

    def fold_vectors(self, dve, chain, spare):
        dve.wait_ge(self.vec_in, self.vec_total)
        for m, n in ((0, P), (1, NS)):
            scale, shift, fold = self.scale[0:n, m, :], self.shift[0:n, m, :], spare[0:n, :]
            chain(dve.scalar_tensor_tensor(fold, scale, 1.0, self.b[0:n, :], ALU.add, ALU.mult))
            chain.mark(dve.tensor_tensor(shift, shift, fold, ALU.add))
            chain(dve.scalar_tensor_tensor(scale, scale, 1.0, self.g[0:n, :], ALU.add, ALU.mult))

    def join(self, dve, chain, t, pieces, y_taken):
        n, v, m = rows(t), t % 2, t // NPT
        x = self.x[0:n, t, :]
        if t == 0:
            dve.wait_ge(self.gate_in, 32)
        dve.wait_ge(self.x_in[t], 16)
        if t >= 2:
            dve.wait_ge(self.rstd_done, t - 1)
        for cols, y, scratch in pieces:
            ins = dve.scalar_tensor_tensor(scratch, self.gate[0:n, m, cols], 1.0, y, ALU.add, ALU.mult)
            if y_taken is None:
                chain(ins)
            else:
                ins.then_inc(y_taken[0], 1)
                y_taken[1] += 1
                dve.wait_ge(*y_taken)
            chain(dve.scalar_tensor_tensor(x[:, cols], x[:, cols], ALPHA, scratch, ALU.mult, ALU.add))
        for c in range(2):
            chain(dve.bn_stats(self.stats[0:n, v, c, :], x[:, c * W:(c + 1) * W]))
        dve.bn_aggr(self.mom[0:n, v, :], self.stats[0:n, v].rearrange("p c s -> p (c s)")).then_inc(self.moments, 1)

    def finish(self, dve, chain, t, h):
        n, v, m = rows(t), t % 2, t // NPT
        x = self.x[0:n, t, :]
        dve.wait_ge(self.moments, t + 1)
        dve.wait_ge(self.rstd_done, t + 1)
        chain(dve.tensor_scalar(x, x, self.mom[0:n, v, 0:1], self.rstd[0:n, v, :], ALU.subtract, ALU.mult))
        if not self.more:
            dve.wait_ge(self.vec_in, self.vec_total)
            dve.tensor_tensor(x, x, self.g[0:n, :], ALU.mult).then_inc(self.xn_used, 1)
            return
        dve.tensor_tensor(h, x, self.scale[0:n, m, :], ALU.mult).then_inc(self.xn_used, 1)
        dve.wait_ge(self.xn_used, t + 1)
        dve.tensor_tensor(h, h, self.shift[0:n, m, :], ALU.add).then_inc(self.h_done, 1)


def mixer_end(core, l, oT, x_from, x_to, hk, logits):
    nc, d, ps = core.nc, core.dram, core.ps
    with Stage(core, f"end{l}") as st:
        extra = st.sb("extra", [P, KD, W])
        scratch = st.sb("scratch", [P, 2, W])
        rw = st.sb("rw", [P, KD, NE])
        r = Residual(core, st, l, 0, True)
        names = ("extra_in", "rw_in", "y_done", "y_taken", "steps", "turned", "kept", "logits_done", "logits_kept")
        s = {n: st.sem(n) for n in names}
        base = core.base[l] + 12
        blocks = [core.ring[:, (base + j) % RING] for j in range(3)] + [extra[:]]

        with nc.Block() as block:
            @block.sync
            def _(sp):
                sp.dma_start(extra[:], core.out_block(l, 3)).then_inc(s["extra_in"], 16)
                sp.dma_start(rw[:], d["router_w"].rearrange("(k p) e -> p k e", p=P)).then_inc(s["rw_in"], 16)
                r.gates(sp)
                r.load(sp, x_from)
                r.vectors(sp)
                for t in range(NT):
                    r.store(sp, t, x_to)
                r.stored(sp)

            @block.tensor
            def _(pe):
                for j in range(3):
                    pe.wait_ge(*core.arrival(base + j))
                pe.wait_ge(s["extra_in"], 16)
                pe.wait_ge(s["rw_in"], 16)

                def route(t):
                    n = rows(t)
                    pe.wait_ge(r.h_done, t + 1)
                    if t:
                        pe.wait_ge(s["kept"], 2 * t)
                    turn_tile(pe, core, hk[:, t, :], t, (4, 5)).then_inc(s["turned"], 1)
                    pe.wait_ge(s["kept"], 2 * (t + 1))
                    if t:
                        pe.wait_ge(s["logits_kept"], t)
                    for k in range(KD):
                        last = pe.matmul(ps[6][0:n, 0:NE], core.hT[:, k, tok(t)], rw[:, k, :],
                                         start=(k == 0), stop=(k == KD - 1))
                    last.then_inc(s["logits_done"], 1)

                for t in range(NT):
                    if t >= 2:
                        pe.wait_ge(s["y_taken"], 2 * (t - 1))
                    for c in range(2):
                        for k in range(2 * KD):
                            last = pe.matmul(ps[2 * (t % 2) + c][0:rows(t), :], oT[:, k, tok(t)],
                                             blocks[2 * (k // KD) + c][:, k % KD, :],
                                             start=(k == 0), stop=(k == 2 * KD - 1))
                        last.then_inc(s["y_done"], 1)
                    if t:
                        route(t - 1)
                route(NT - 1)

            @block.vector
            def _(dve):
                chain = Chain(dve, s["steps"])
                chain(dve.memset(logits[:], 0.0))
                taken = [s["y_taken"], 0]
                r.fold_vectors(dve, chain, scratch[:].rearrange("p c n -> p (c n)"))
                for t in range(NT):
                    n = rows(t)
                    dve.wait_ge(s["y_done"], 2 * (t + 1))
                    r.join(dve, chain, t, [(slice(c * W, (c + 1) * W), ps[2 * (t % 2) + c][0:n, :], scratch[0:n, c, :])
                                           for c in range(2)], taken)
                    r.finish(dve, chain, t, hk[0:n, t, :])

            @block.gpsimd
            def _(pool):
                r.pchain = Chain(pool, r.psteps)
                for t in range(NT):
                    r.deviation(pool, t)
                    r.outputs(pool, t)

            @block.scalar
            def _(act):
                act.wait_ge(s["steps"], 1)
                for t in range(NT):
                    act.wait_ge(s["turned"], t + 1)
                    keep_turned(act, core, t, (4, 5), s["kept"])
                    act.wait_ge(s["logits_done"], t + 1)
                    act.activation(logits[0:rows(t), t, :], ps[6][0:rows(t), 0:NE], ACT.Copy
                                   ).then_inc(s["logits_kept"], 1)


_OUTS = [((1, SEQ, D), "float32"), ((DECB, DECL, D), "float32"),
         ((1, 1, 4, DK, DV), "float32"), ((1, DECB, 4, DK, DV), "float32"),
         ((1, 1, 16, P, P), "float32"), ((1, DECB, 16, P, P), "float32"),
         ((1, 1, 3, 4096), "float32"), ((1, DECB, 3, 4096), "float32")]


def constants():
    f = np.float32
    i = np.arange(P)
    c = {"c_ident": np.eye(P, dtype=f), "c_fold": np.zeros((P, 1 + DECB), f)}
    for m in range(1 + DECB):
        c["c_fold"][m::32, m] = 1
    c["c_eps"] = np.tile(np.array([LN_EPS, RMS_EPS, P * RMS_EPS, -0.5], f), (P, 1))
    inv = np.power(f(10000.0), -np.linspace(0.0, 1.0, P, dtype=f)).astype(f)
    pos = np.zeros((P, NT), f)
    for t in range(NPT):
        pos[:, t] = P * t + i
    pos[:NS, NPT] = 4096 + np.arange(NS) % DECL
    ang = (pos[:, :, None] * inv[None, None, :]).astype(f)
    c["c_cos"], c["c_sin"] = np.cos(ang).astype(f), np.sin(ang).astype(f)
    lg = np.log(1.0 - 2.0 ** (-5.0 - np.arange(HEADS)))
    ks = DK ** -0.5
    diff = i[None, :] - i[:, None]
    c["c_dec"] = np.stack([np.where(diff >= 0, np.exp(np.maximum(diff, 0) * g), 0) * ks for g in lg], 1).astype(f)
    s = np.arange(NS)
    ds = s[None, :] - s[:, None]
    same = (s[None, :] // DECL == s[:, None] // DECL)
    c["c_dec_s"] = np.stack([np.where((ds >= 0) & same, np.exp(np.maximum(ds, 0) * g), 0) * ks for g in lg], 1).astype(f)
    q = np.concatenate([i + 1.0, s % DECL + 1.0])
    c["c_qdec"] = np.tile(np.exp(q[None, :] * lg[:, None])[None], (P, 1, 1)).astype(f)
    c["c_kdec"] = (np.exp((P - 1.0 - i)[:, None] * lg[None, :]) * ks).astype(f)
    own = (s[:, None] // DECL == np.arange(DECB)[None, :])
    c["c_kdec_s"] = (np.exp((DECL - 1.0 - s % DECL)[:, None] * lg[None, :])[:, :, None] * own[:, None, :] * ks).astype(f)
    c["c_sdec"] = np.tile(np.stack([np.exp(P * lg), np.exp(DECL * lg)])[None], (P, 1, 1)).astype(f)
    c["c_seqmask"] = np.tile(own.T[None], (P, 1, 1)).astype(f)
    c["c_strict"] = (i[:, None] < i[None, :]).astype(f)
    c["c_cw4"] = np.tile(np.arange(4, 0, -1, dtype=f), (P, 1))
    c["c_cw16"] = np.tile(np.arange(NE, 0, -1, dtype=f), (P, 1))
    c["c_thr"] = np.tile(P * np.arange(NT, dtype=f), (P, 1))
    e = np.arange(NE)
    c["c_before"] = np.tile((e[None, :] < e[:, None])[None], (P, 1, 1)).astype(f)
    c["c_tiles"] = np.tile(np.arange(MAXT, dtype=f), (P, 1))
    c["c_rowmask"] = np.ones((P, NT), f)
    c["c_rowmask"][NS:, NPT] = 0
    c["c_own"] = own.astype(f)
    c["c_incl"] = (i[:, None] <= i[None, :]).astype(f)
    c["c_incl_s"] = ((s[:, None] <= s[None, :]) & same).astype(f)
    c["c_same"] = same.astype(f)
    c["c_lower"] = (i[None, :] < i[:, None]).astype(f)
    c["c_lower_s"] = ((s[None, :] < s[:, None]) & same).astype(f)
    lv = []
    for b in (1, 2, 4, 8, 16, 32, 64):
        lv.append((i[:, None] // (2 * b) == i[None, :] // (2 * b)) & (i[:, None] // b % 2 == 1) & (i[None, :] // b % 2 == 0))
    c["c_levels"] = np.stack([m.T for m in lv] + [lv[0]], 1).astype(f)
    c["c_qscale"] = np.tile(np.array([P, P, 1, 1], f), (P, 1))
    return c


_NAMES = ["x_prompt", "x_sample", "state_ret", "state_dn", "state_conv", "c_prompt", "c_sample", "w_ada", "b_ada",
          "ln_g", "ln_b", "ret_w_in", "ret_gn_g", "ret_w_out", "dn_w_in", "dn_conv_w", "dn_a_log", "dn_dt_bias",
          "dn_norm_g", "dn_w_out", "router_w", "router_b", "moe_w_gu", "moe_w_down"]


def build(nc, names, args, outs):
    d = dict(zip(names, args))
    (d["y_p"], d["y_s"], d["ret_p"], d["ret_s"], d["dn_p"], d["dn_s"], d["conv_p"], d["conv_s"]) = outs
    d["mod"] = nc.dram_tensor("mod_rows", [1 + DECB, 2 * MODW], F32).ap()
    d["oT"] = nc.dram_tensor("oT_spill", [P, 16, NTOK], F32).ap()
    for name in ("x1", "x2", "x3"):
        x = nc.dram_tensor(name + "_rows", [NTOK, D], F32).ap()
        d[name] = lambda t, x=x: x[tok(t), :]
    d["rows"] = nc.dram_tensor("expert_rows", [MAXT * P, D], F32).ap()
    d["y_rows"] = nc.dram_tensor("expert_outputs", [MAXT * P, D], F32).ap()
    xp = d["x_prompt"].rearrange("o s d -> (o s) d")
    xs = d["x_sample"].rearrange("b s d -> (b s) d")
    d["x0"] = lambda t: xp[P * t:P * (t + 1), :] if t < NPT else xs
    wi = d["ret_w_in"][0].rearrange("(k p) n -> p k n", p=P)
    wo = [d[n][0].rearrange("(k p) n -> p k n", p=P) for n in ("ret_w_out", "dn_w_out")]
    every = slice(0, KD)
    ret = []
    for h in range(HEADS):
        ret.append([(every, slice(0, W), wi[:, :, 2048 + W * h:2048 + W * (h + 1)])])
        ret.append([(every, slice(0, W), wi[:, :, 4096 + W * h:4096 + W * (h + 1)])])
        ret.append([(every, slice(0, DK), wi[:, :, DK * h:DK * (h + 1)]),
                    (every, slice(DK, W), wi[:, :, 1024 + DK * h:1024 + DK * (h + 1)])])
    d["mixer_blocks"] = []
    for l in range(2):
        d["mixer_blocks"].append((ret if l == 0 else d_dn(d)) + [
            [(every, slice(0, W), wo[l][:, 8 * (j // 2):8 * (j // 2) + 8, W * (j % 2):W * (j % 2) + W])] for j in range(3)])
    with ExitStack() as ctx:
        core = Core(nc, ctx, d)
        core.out_block = lambda l, j: wo[l][:, 8 * (j // 2):8 * (j // 2) + 8, W * (j % 2):W * (j % 2) + W]
        setup_and_modulation(core)
        first_features(core)
        with ExitStack() as mid:
            core.oT = core.sb(mid, "oT", [P, 16, NTOK])
            retention(core)
            moe_half(core, 0, mid, d["x0"], d["x1"], d["x2"], True)
        with ExitStack() as mid:
            tables = Gates(core, mid)
            masks = {"incl": core.sb(mid, "incl", [P, P]), "lower": core.sb(mid, "lower", [P, P]),
                     "incl_s": core.sb(mid, "incl_s", [NS, NS]), "lower_s": core.sb(mid, "lower_s", [NS, NS]),
                     "same": core.sb(mid, "same", [NS, NS]), "levels": core.sb(mid, "levels", [P, 8, P]),
                     "qscale": core.sb(mid, "qscale", [P, 4]), "own": core.sb(mid, "own", [NS, DECB])}
            delta_gates(core, tables, masks)
            delta(core, tables, masks)
        with ExitStack() as mid:
            core.oT = core.sb(mid, "oT2", [P, 16, NTOK])
            with Stage(core, "oTin") as st:
                q = st.sem("q")
                with nc.Block() as block:
                    @block.sync
                    def _(sp):
                        sp.dma_start(core.oT[:], d["oT"]).then_inc(q, 16)
                        sp.wait_ge(q, 16)
            y_to = lambda t: d["y_p"].rearrange("o s d -> (o s) d")[tok(t), :] if t < NPT else d["y_s"].rearrange("b s d -> (b s) d")
            moe_half(core, 1, mid, d["x2"], d["x3"], y_to, False)


def moe_half(core, l, mid, x_from, x_mid, x_to, more):
    d = core.dram
    hk = core.sb(mid, f"hk{l}", [P, NT, D])
    logits = core.sb(mid, f"logits{l}", [P, NT, NE])
    mixer_end(core, l, core.oT, x_from, x_mid, hk, logits)
    plan = Plan(core, mid, l)
    routing(core, l, hk, logits, plan)
    experts(core, l, plan)
    combine(core, l, plan, x_mid, x_to, more)


def d_dn(d):
    wi = d["dn_w_in"][0].rearrange("(k p) n -> p k n", p=P)
    every, out = slice(0, KD), []
    for g in range(HEADS):
        out.append([(every, slice(0, W), wi[:, :, 2048 + W * g:2048 + W * (g + 1)])])
        out.append([(every, slice(0, DE), wi[:, :, DE * g:DE * (g + 1)]),
                    (every, slice(DE, W), wi[:, :, 1024 + DE * g:1024 + DE * (g + 1)])])
        out.append([(every, slice(0, W), wi[:, :, 4096 + W * g:4096 + W * (g + 1)])])
    return out


def kernel(**inputs):
    import numpy as _np
    import concourse.bacc as _bacc
    from concourse import mybir as _mybir
    from concourse.bass_utils import run_bass_kernel_spmd as _run

    nc = _bacc.Bacc("TRN2", target_bir_lowering=False, num_devices=1)
    given = {name: inputs[name] for name in _NAMES}
    given.update(constants())
    arrays, args = {}, []
    for name, value in given.items():
        a = _np.ascontiguousarray(value)
        arrays[f"in_{name}_dram"] = a
        args.append(nc.dram_tensor(f"in_{name}_dram", a.shape, _mybir.dt.from_np(a.dtype), kind="ExternalInput").ap())
    outs = []
    for i, (shape, dtype) in enumerate(_OUTS):
        dt = _mybir.dt.from_np(_np.dtype(dtype))
        outs.append(nc.dram_tensor(f"out_{i}_dram", shape, dt, kind="ExternalOutput").ap())
    build(nc, list(given), args, outs)
    r = _run(nc, [arrays], core_ids=[0])
    return tuple(r.results[0][f"out_{i}_dram"] for i in range(len(_OUTS)))
```
